# Optimizing a Trainium2 kernel written in Bass

```python
import jax, jax.numpy as jnp
from jax import lax
import numpy as np
import jax
import jax.numpy as jnp
import math

D_MODEL = 1024
BATCH = 1
SEQ = 512
DEPTH = 2

GRID_W = 64
CTX_LEN = 256
N_MIXERS = 2
EXPAND = 2
E_WIDTH = EXPAND * D_MODEL
HEAD_K = 128
N_HEADS = E_WIDTH // HEAD_K
HEAD_V = E_WIDTH // N_HEADS
CHUNK = 16
CONV_W = 31
EPS = 1e-6


def _rmsnorm(x, g):
    xf = x.astype(jnp.float32)
    y = xf * lax.rsqrt(jnp.mean(xf * xf, axis=-1, keepdims=True) + EPS)
    return (y * g.astype(jnp.float32)).astype(x.dtype)

def _layernorm(x, g, b):
    xf = x.astype(jnp.float32)
    xc = xf - jnp.mean(xf, axis=-1, keepdims=True)
    var = jnp.mean(xc * xc, axis=-1, keepdims=True)
    return (xc * lax.rsqrt(var + EPS) * g.astype(jnp.float32) + b.astype(jnp.float32)).astype(x.dtype)

def _ada(cvec, w, b):
    m = jax.nn.silu(cvec) @ w + b
    return jnp.split(m, 3, axis=-1)

def _modulate(x, g, shift, scale):
    return _rmsnorm(x, g) * (1 + scale) + shift

def _hgrn_lower_bounds(lb_logits):
    p = jax.nn.softmax(lb_logits.astype(jnp.float32), axis=1)
    return jnp.cumsum(p, axis=1) - p[:, :1]

def _heads(t):
    return t.reshape(t.shape[0], t.shape[1], N_HEADS, -1).astype(jnp.float32)

def _forget(z, lb):
    f = lb + (1 - lb) * jax.nn.sigmoid(z.astype(jnp.float32))
    return _heads(jnp.log(f)), _heads(1 - f)

def _chunk_gla(q, k, v, g, s0):
    b_, length, h_, _ = q.shape
    n = length // CHUNK

    def to_chunks(t):
        return t.reshape(b_, n, CHUNK, h_, t.shape[-1]).transpose(1, 0, 3, 2, 4)

    mask = jnp.tril(jnp.ones((CHUNK, CHUNK), dtype=bool))
    mid = CHUNK // 2

    def step(state, inp):
        qc, kc, vc, gc = inp
        bcum = jnp.cumsum(gc, axis=-2)
        b_ref = bcum[..., mid:mid + 1, :]
        b_end = bcum[..., -1:, :]
        inter = jnp.einsum('bhck,bhkv->bhcv', qc * jnp.exp(bcum), state)
        scores = jnp.einsum('bhtk,bhsk->bhts', qc * jnp.exp(bcum - b_ref), kc * jnp.exp(b_ref - bcum))
        intra = jnp.einsum('bhts,bhsv->bhtv', jnp.where(mask, scores, 0.0), vc)
        new_state = (jnp.exp(b_end[..., 0, :])[..., None] * state
                     + jnp.einsum('bhsk,bhsv->bhkv', kc * jnp.exp(b_end - bcum), vc))
        return new_state, inter + intra

    s_final, o = lax.scan(step, s0, (to_chunks(q), to_chunks(k), to_chunks(v), to_chunks(g)))
    o = o.transpose(1, 0, 3, 2, 4).reshape(b_, length, h_, v.shape[-1])
    return o, s_final

def _chunk_gla_rev(q, k, v, g, s0):
    flip = lambda t: jnp.flip(t, axis=1)
    o, s_final = _chunk_gla(flip(q), flip(k), flip(v), flip(g), s0)
    return flip(o), s_final

def _hgrn_project(h, w_in, lb_f, lb_b):
    p = h @ w_in
    q, v, zf, zb, gate = jnp.split(p, 5, axis=-1)
    gf, kf = _forget(zf, lb_f)
    gb, kb = _forget(zb, lb_b)
    return _heads(jax.nn.silu(q)), _heads(v), gf, kf, gb, kb, gate

def _hgrn_readout(o, gate, norm_g, w_out):
    o = _rmsnorm(o, norm_g)
    o = o.reshape(o.shape[0], o.shape[1], E_WIDTH).astype(gate.dtype)
    return (o * jax.nn.silu(gate)) @ w_out

def _hgrn2_mixer(h, hc, w_in, lb_f, lb_b, norm_g, w_out, need_ctx):
    q, v, gf, kf, gb, kb, gate = _hgrn_project(h, w_in, lb_f, lb_b)
    qc, vc, gfc, kfc, gbc, kbc, gatec = _hgrn_project(hc, w_in, lb_f, lb_b)
    s0 = jnp.zeros((hc.shape[0], N_HEADS, HEAD_K, HEAD_V), jnp.float32)
    oc_f, sc_f = _chunk_gla(qc, kfc, vc, gfc, s0)
    oc_b, sc_b = _chunk_gla_rev(qc, kbc, vc, gbc, s0)
    o_f, _ = _chunk_gla(q, kf, v, gf, sc_f)
    o_b, _ = _chunk_gla_rev(q, kb, v, gb, sc_b)
    y = _hgrn_readout(o_f + o_b, gate, norm_g, w_out)
    yc = _hgrn_readout(oc_f + oc_b, gatec, norm_g, w_out) if need_ctx else None
    return y, yc

def _dwconv(u, w, b):
    pad = CONV_W // 2
    out = lax.conv_general_dilated(u, w[:, None, :], window_strides=(1,), padding=[(pad, pad)],
                                   dimension_numbers=('NWC', 'WIO', 'NWC'),
                                   feature_group_count=u.shape[-1])
    return out + b

def _latent_dwconv(u, w, b, vertical):
    b_, length, ch = u.shape
    rows = length // GRID_W
    grid = u.reshape(b_, rows, GRID_W, ch)
    if vertical:
        grid = grid.transpose(0, 2, 1, 3)
    n1, n2 = grid.shape[1], grid.shape[2]
    out = _dwconv(grid.reshape(b_ * n1, n2, ch), w, b).reshape(b_, n1, n2, ch)
    if vertical:
        out = out.transpose(0, 2, 1, 3)
    return out.reshape(b_, length, ch)

def _conv_mixer(h, w_in, b_in, dw, dw_b, ln_g, ln_b, w_out, b_out, conv_fn):
    p = h @ w_in + b_in
    a, gl, gate = jnp.split(p, 3, axis=-1)
    u = a * jax.nn.sigmoid(gl)
    u = conv_fn(u, dw, dw_b)
    u = jax.nn.silu(_layernorm(u, ln_g, ln_b))
    return (u * jax.nn.silu(gate)) @ w_out + b_out

def first_inputs(seed: int = 0) -> dict:
    key = jax.random.key(seed)
    ks = jax.random.split(key, 20)
    n_a = (DEPTH + 1) // 2
    n_b = DEPTH // 2
    f32 = jnp.float32

    def w(k, shape, fan_in):
        return jax.random.normal(k, shape, f32) * fan_in ** -0.5

    def small(k, shape, s=0.02):
        return jax.random.normal(k, shape, f32) * s

    return {
        "x": jax.random.normal(ks[0], (BATCH, SEQ, D_MODEL), f32),
        "c": jax.random.normal(ks[1], (BATCH, D_MODEL), f32),
        "ctx": jax.random.normal(ks[2], (BATCH, CTX_LEN, D_MODEL), f32),
        "c_ctx": jax.random.normal(ks[3], (D_MODEL,), f32),
        "norm_g": 1.0 + small(ks[4], (DEPTH, D_MODEL)),
        "ada_w": w(ks[5], (DEPTH, D_MODEL, 3 * D_MODEL), D_MODEL),
        "ada_b": small(ks[6], (DEPTH, 3 * D_MODEL)),
        "hgrn_w_in": w(ks[7], (n_a, D_MODEL, 5 * E_WIDTH), D_MODEL),
        "hgrn_lb_logits": small(ks[8], (2, n_a, E_WIDTH), 0.1),
        "hgrn_norm_g": 1.0 + small(ks[9], (n_a, HEAD_V)),
        "hgrn_w_out": w(ks[10], (n_a, E_WIDTH, D_MODEL), E_WIDTH),
        "conv_w_in": w(ks[11], (n_b, D_MODEL, 3 * E_WIDTH), D_MODEL),
        "conv_b_in": small(ks[12], (n_b, 3 * E_WIDTH)),
        "conv_dw": w(ks[13], (n_b, CONV_W, E_WIDTH), CONV_W),
        "conv_dw_b": small(ks[14], (n_b, E_WIDTH)),
        "conv_ln_g": 1.0 + small(ks[15], (n_b, E_WIDTH)),
        "conv_ln_b": small(ks[16], (n_b, E_WIDTH)),
        "conv_w_out": w(ks[17], (n_b, E_WIDTH, D_MODEL), E_WIDTH),
        "conv_b_out": small(ks[18], (n_b, D_MODEL)),
        "final_norm_g": 1.0 + small(ks[19], (D_MODEL,)),
    }

def first_block(x, c, ctx, c_ctx, norm_g, ada_w, ada_b, hgrn_w_in, hgrn_lb_logits, hgrn_norm_g, hgrn_w_out,
              conv_w_in, conv_b_in, conv_dw, conv_dw_b, conv_ln_g, conv_ln_b, conv_w_out, conv_b_out,
              final_norm_g):
    lb = _hgrn_lower_bounds(hgrn_lb_logits)
    for i in range(DEPTH):
        mixer = i % N_MIXERS
        j = i // N_MIXERS
        need_ctx = any(m % N_MIXERS == 0 for m in range(i + 1, DEPTH))
        shift, scale, gate = _ada(c, ada_w[i], ada_b[i])
        h = _modulate(x, norm_g[i], shift[:, None], scale[:, None])
        if mixer == 0 or need_ctx:
            shift_c, scale_c, gate_c = _ada(c_ctx, ada_w[i], ada_b[i])
            hc = _modulate(ctx, norm_g[i], shift_c, scale_c)
        if mixer == 0:
            y, yc = _hgrn2_mixer(h, hc, hgrn_w_in[j], lb[0, j], lb[1, j], hgrn_norm_g[j], hgrn_w_out[j], need_ctx)
        else:
            vertical = (j % 2 == 1)
            lat_conv = lambda u, dw, dwb: _latent_dwconv(u, dw, dwb, vertical)
            y = _conv_mixer(h, conv_w_in[j], conv_b_in[j], conv_dw[j], conv_dw_b[j], conv_ln_g[j], conv_ln_b[j],
                            conv_w_out[j], conv_b_out[j], lat_conv)
            yc = (_conv_mixer(hc, conv_w_in[j], conv_b_in[j], conv_dw[j], conv_dw_b[j], conv_ln_g[j], conv_ln_b[j],
                              conv_w_out[j], conv_b_out[j], _dwconv) if need_ctx else None)
        x = x + gate[:, None] * y
        if need_ctx:
            ctx = ctx + gate_c * yc
    return _rmsnorm(x, final_norm_g)


_first_inputs = first_inputs


def first_inputs(seed=0):
    import zlib

    import numpy as np

    out = dict(_first_inputs(seed))
    spreads = {}
    factors = {}
    for name, (base, spread) in spreads.items():
        noise = np.random.default_rng([zlib.crc32(name.encode()), seed]).standard_normal(out[name].shape)
        drawn = base * np.exp(spread * noise) if base else spread * noise
        out[name] = __import__('jax').numpy.asarray(drawn.astype(out[name].dtype))
    for name, factor in factors.items():
        out[name] = (out[name] * factor).astype(out[name].dtype)
    return out


_narrow_inputs = first_inputs


def first_inputs(seed=0):

    out = dict(_narrow_inputs(seed))
    wider = {'ctx': 8.81,
     'c_ctx': 9.73,
     'norm_g': 5.02,
     'hgrn_norm_g': 6.29,
     'conv_b_in': 10.69,
     'conv_dw_b': 8.26,
     'conv_ln_g': 9.41,
     'conv_ln_b': 11.87,
     'conv_b_out': 6.23,
     'final_norm_g': 3.16}
    for name, times in wider.items():
        mean = out[name].mean()
        out[name] = (mean + times * (out[name] - mean)).astype(out[name].dtype)
    return out


DEPTH_2 = 1

GM_W = 512
GM_GROUPS = 4
GM_CHUNK = 128
ML_H = 4
ML_DH = 128
ML_W = ML_H * ML_DH
ML_CHUNK = 64
CONV_K = 4
NSA_H = 8
NSA_G = 2
NSA_R = NSA_H // NSA_G
NSA_DH = 64
NSA_W = NSA_H * NSA_DH
NSA_KV = NSA_G * NSA_DH
NSA_NB = 3
CMP_BLOCK = 32
CMP_STRIDE = 16
SEL_BLOCK = 64
TOP_N = 8
WINDOW = 512
NSA_QC = 32
N_BRANCH = 3
D_FF = 4 * D_MODEL
NEG = -1e30
BIG = 1e4
F32 = jnp.float32
SPLIT_SIZES = (GM_W, GM_W, ML_W, ML_W, ML_W, ML_W, ML_H, ML_H, NSA_W, NSA_KV, NSA_KV, NSA_KV, NSA_KV, NSA_KV, NSA_KV, NSA_H * NSA_NB, D_MODEL, D_MODEL, D_MODEL)
P_TOTAL = sum(SPLIT_SIZES)


def rms_norm(x, g):
    x32 = x.astype(F32)
    y = x32 * lax.rsqrt(jnp.mean(x32 * x32, axis=-1, keepdims=True) + EPS)
    return (y * g.astype(F32)).astype(x.dtype)

def layer_norm(x, g, b):
    x32 = x.astype(F32)
    mu = jnp.mean(x32, axis=-1, keepdims=True)
    var = jnp.mean(jnp.square(x32 - mu), axis=-1, keepdims=True)
    return ((x32 - mu) * lax.rsqrt(var + EPS) * g.astype(F32) + b.astype(F32)).astype(x.dtype)

def causal_conv(x, w, b):
    S = x.shape[1]
    xp = jnp.pad(x, ((0, 0), (CONV_K - 1, 0), (0, 0)))
    y = b
    for j in range(CONV_K):
        y = y + xp[:, j:j + S] * w[j]
    return y

def gmlp_mixer(u_pre, v_pre, ln_g, ln_b, ws, bs):
    B, S, _ = u_pre.shape
    u = jax.nn.gelu(u_pre)
    v = layer_norm(jax.nn.gelu(v_pre), ln_g, ln_b)
    dg = GM_W // GM_GROUPS
    v = v.reshape(B, S // GM_CHUNK, GM_CHUNK, GM_GROUPS, dg)
    w = ws * jnp.tril(jnp.ones((GM_CHUNK, GM_CHUNK), ws.dtype))
    mixed = jnp.einsum('gts,bcsgd->bctgd', w, v) + bs.T[:, :, None]
    return u * mixed.reshape(B, S, GM_W)

def mlstm_chunk_step(carry, xs):
    c_mat, n_vec, m_prev = carry
    q, k, v, ig, lf = xs
    L = q.shape[2]
    tril = jnp.tril(jnp.ones((L, L), dtype=bool))
    b = jnp.cumsum(lf, axis=-1)
    a = b + m_prev[..., None]
    d = jnp.where(tril, b[..., :, None] - b[..., None, :] + ig[..., None, :], -jnp.inf)
    m = jnp.maximum(a, jnp.max(d, axis=-1))
    w_inter = jnp.exp(a - m)
    s = jnp.einsum('bhtd,bhsd->bhts', q, k) * jnp.exp(d - m[..., None])
    num = jnp.einsum('bhts,bhse->bhte', s, v) + w_inter[..., None] * jnp.einsum('bhed,bhtd->bhte', c_mat, q)
    den = jnp.sum(s, axis=-1) + w_inter * jnp.einsum('bhd,bhtd->bht', n_vec, q)
    h = num / jnp.maximum(jnp.abs(den), jnp.exp(-m))[..., None]
    m_last = m[..., -1]
    w_prev = jnp.exp(a[..., -1] - m_last)
    w_s = jnp.exp(b[..., -1:] - b + ig - m_last[..., None])
    c_new = w_prev[..., None, None] * c_mat + jnp.einsum('bhs,bhse,bhsd->bhed', w_s, v, k)
    n_new = w_prev[..., None] * n_vec + jnp.einsum('bhs,bhsd->bhd', w_s, k)
    return (c_new, n_new, m_last), h

def mlstm_mixer(q, k, v, o_pre, i_pre, f_pre, conv_w, conv_b, gate_b, norm_g):
    B, S, _ = v.shape
    dtype = v.dtype
    qk = jax.nn.silu(causal_conv(jnp.concatenate([q, k], axis=-1), conv_w, conv_b))
    q, k = jnp.split(qk, 2, axis=-1)
    nc = S // ML_CHUNK

    def heads(t):
        return t.astype(F32).reshape(B, nc, ML_CHUNK, ML_H, ML_DH).transpose(1, 0, 3, 2, 4)

    def gate_heads(t):
        return t.reshape(B, nc, ML_CHUNK, ML_H).transpose(1, 0, 3, 2)

    qh = heads(q)
    kh = heads(k) * (ML_DH ** -0.5)
    vh = heads(v)
    ig = gate_heads((i_pre + gate_b[:ML_H]).astype(F32))
    lf = gate_heads(jax.nn.log_sigmoid((f_pre + gate_b[ML_H:]).astype(F32)))
    init = (jnp.zeros((B, ML_H, ML_DH, ML_DH), F32), jnp.zeros((B, ML_H, ML_DH), F32), jnp.zeros((B, ML_H), F32))
    _, h = lax.scan(mlstm_chunk_step, init, (qh, kh, vh, ig, lf))
    h = h.transpose(1, 0, 3, 2, 4).reshape(B, S, ML_H, ML_DH)
    mu = jnp.mean(h, axis=-1, keepdims=True)
    var = jnp.mean(jnp.square(h - mu), axis=-1, keepdims=True)
    hn = (h - mu) * lax.rsqrt(var + EPS) * norm_g.astype(F32).reshape(ML_H, ML_DH)
    return (jax.nn.sigmoid(o_pre.astype(F32)) * hn.reshape(B, S, ML_W)).astype(dtype)

def compress_blocks(kv, pe, w1, w2):
    B, S, G, dh = kv.shape
    n_cmp = (S - CMP_BLOCK) // CMP_STRIDE + 1
    idx = jnp.arange(n_cmp)[:, None] * CMP_STRIDE + jnp.arange(CMP_BLOCK)[None, :]
    blocks = kv[:, idx] + pe[:, None, :]
    blocks = blocks.transpose(0, 3, 1, 2, 4).reshape(B, G, n_cmp, CMP_BLOCK * dh)
    return jax.nn.gelu(blocks @ w1) @ w2

def masked_softmax(s, valid, axis=-1):
    p = jax.nn.softmax(jnp.where(valid, s, NEG), axis=axis)
    return jnp.where(valid, p, 0.0)

def nsa_mixer(q, kc, vc, ks, vs, kw, vw, gates, pe_k, pe_v, phi_k1, phi_k2, phi_v1, phi_v2):
    B, S, _ = q.shape
    dtype = q.dtype
    qh = q.reshape(B, S, NSA_G, NSA_R, NSA_DH).transpose(0, 2, 3, 1, 4)

    def kv_heads(t):
        return t.reshape(B, S, NSA_G, NSA_DH)

    k_cmp = compress_blocks(kv_heads(kc), pe_k, phi_k1, phi_k2)
    v_cmp = compress_blocks(kv_heads(vc), pe_v, phi_v1, phi_v2).astype(F32)
    n_cmp = k_cmp.shape[2]
    cmp_start = jnp.arange(n_cmp) * CMP_STRIDE
    cmp_end = cmp_start + CMP_BLOCK - 1
    cmp_center = cmp_start.astype(F32) + (CMP_BLOCK - 1) * 0.5
    n_sel = S // SEL_BLOCK
    top_n = min(TOP_N, n_sel)
    sel = jnp.arange(n_sel)
    overlap = ((cmp_start[:, None] <= sel[None, :] * SEL_BLOCK + SEL_BLOCK - 1) & (cmp_end[:, None] >= sel[None, :] * SEL_BLOCK)).astype(F32)
    k_sel = kv_heads(ks).transpose(0, 2, 1, 3).reshape(B, NSA_G, n_sel, SEL_BLOCK, NSA_DH)
    v_sel = kv_heads(vs).transpose(0, 2, 1, 3).reshape(B, NSA_G, n_sel, SEL_BLOCK, NSA_DH)
    pad = ((0, 0), (0, 0), (WINDOW, 0), (0, 0))
    k_win = jnp.pad(kv_heads(kw).transpose(0, 2, 1, 3), pad)
    v_win = jnp.pad(kv_heads(vw).transpose(0, 2, 1, 3), pad)
    g = jax.nn.sigmoid(gates.astype(F32)).reshape(B, S, NSA_G, NSA_R, NSA_NB).transpose(0, 2, 3, 1, 4)
    slopes = (2.0 ** (-8.0 * (jnp.arange(NSA_H, dtype=F32) + 1.0) / NSA_H)).reshape(NSA_G, NSA_R)
    scale = NSA_DH ** -0.5
    bi = jnp.arange(B)[:, None, None, None]
    gi = jnp.arange(NSA_G)[None, :, None, None]

    def query_chunk(qi):
        t0 = qi * NSA_QC
        qb = lax.dynamic_slice_in_dim(qh, t0, NSA_QC, axis=3)
        t = t0 + jnp.arange(NSA_QC)
        tf = t.astype(F32)
        sc = jnp.einsum('bgrqd,bgcd->bgrqc', qb, k_cmp).astype(F32) * scale - slopes[:, :, None, None] * (tf[:, None] - cmp_center[None, :])
        p_c = masked_softmax(sc, cmp_end[None, :] <= t[:, None])
        o_cmp = jnp.einsum('bgrqc,bgcd->bgrqd', p_c, v_cmp)
        imp = jnp.einsum('bgrqc,cj->bgqj', p_c, overlap)
        jt = (t // SEL_BLOCK)[:, None]
        forced = (sel == 0) | (sel == jt) | (sel == jt - 1)
        imp = jnp.where(sel > jt, NEG, jnp.where(forced, BIG, imp))
        _, idx = lax.top_k(imp, top_n)
        kg = k_sel[bi, gi, idx]
        vg = v_sel[bi, gi, idx].astype(F32)
        s_pos = idx[..., None] * SEL_BLOCK + jnp.arange(SEL_BLOCK)
        dist_s = (tf[:, None, None] - s_pos.astype(F32))[:, :, None]
        ss = jnp.einsum('bgrqd,bgqnld->bgrqnl', qb, kg).astype(F32) * scale - slopes[:, :, None, None, None] * dist_s
        p_s = masked_softmax(ss, (s_pos <= t[:, None, None])[:, :, None], axis=(-2, -1))
        o_sel = jnp.einsum('bgrqnl,bgqnld->bgrqd', p_s, vg)
        kwb = lax.dynamic_slice_in_dim(k_win, t0, WINDOW + NSA_QC, axis=2)
        vwb = lax.dynamic_slice_in_dim(v_win, t0, WINDOW + NSA_QC, axis=2).astype(F32)
        pos = t0 - WINDOW + jnp.arange(WINDOW + NSA_QC)
        sw = jnp.einsum('bgrqd,bgkd->bgrqk', qb, kwb).astype(F32) * scale - slopes[:, :, None, None] * (tf[:, None] - pos.astype(F32)[None, :])
        valid_w = (pos[None, :] >= 0) & (pos[None, :] <= t[:, None]) & (t[:, None] - pos[None, :] < WINDOW)
        o_win = jnp.einsum('bgrqk,bgkd->bgrqd', masked_softmax(sw, valid_w), vwb)
        gb = lax.dynamic_slice_in_dim(g, t0, NSA_QC, axis=3)
        return gb[..., 0:1] * o_cmp + gb[..., 1:2] * o_sel + gb[..., 2:3] * o_win

    out = lax.map(query_chunk, jnp.arange(S // NSA_QC))
    return out.transpose(1, 0, 4, 2, 3, 5).reshape(B, S, NSA_W).astype(dtype)

def hybrid_mixer(h, w_in, gm_ln_g, gm_ln_b, gm_ws, gm_bs, ml_conv_w, ml_conv_b, ml_gate_b, ml_norm_g,
                 nsa_pe_k, nsa_pe_v, nsa_phi_k1, nsa_phi_k2, nsa_phi_v1, nsa_phi_v2, w_up_a, w_up_b, w_up_c, w_out):
    z = h @ w_in
    (gu, gv, mq, mk, mv, mo, mi, mf, nq, nkc, nvc, nks, nvs, nkw, nvw, ngate, ga, gbr, gc) = jnp.split(
        z, np.cumsum(SPLIT_SIZES)[:-1].tolist(), axis=-1)
    y_a = gmlp_mixer(gu, gv, gm_ln_g, gm_ln_b, gm_ws, gm_bs) @ w_up_a
    y_b = mlstm_mixer(mq, mk, mv, mo, mi, mf, ml_conv_w, ml_conv_b, ml_gate_b, ml_norm_g) @ w_up_b
    y_c = nsa_mixer(nq, nkc, nvc, nks, nvs, nkw, nvw, ngate, nsa_pe_k, nsa_pe_v,
                    nsa_phi_k1, nsa_phi_k2, nsa_phi_v1, nsa_phi_v2) @ w_up_c
    merged = jax.nn.sigmoid(ga) * y_a + jax.nn.sigmoid(gbr) * y_b + jax.nn.sigmoid(gc) * y_c
    return merged @ w_out

def second_inputs(seed: int = 0) -> dict:
    key = jax.random.key(seed)
    ks = jax.random.split(key, 40)
    L = DEPTH_2

    def nrm(k, shape, scale):
        return scale * jax.random.normal(k, shape, F32)

    ml_gate_b = jnp.concatenate([nrm(ks[12], (L, ML_H), 0.1),
                                 jnp.linspace(3.0, 6.0, ML_H, dtype=F32)[None, :] + nrm(ks[13], (L, ML_H), 0.1)], axis=-1)
    return {
        'x': nrm(ks[0], (BATCH, SEQ, D_MODEL), 1.0),
        'c': nrm(ks[1], (BATCH, D_MODEL), 1.0),
        'g_norm1': 1.0 + nrm(ks[2], (L, D_MODEL), 0.02),
        'g_norm2': 1.0 + nrm(ks[3], (L, D_MODEL), 0.02),
        'w_ada': nrm(ks[4], (L, D_MODEL, 6 * D_MODEL), 0.3 * D_MODEL ** -0.5),
        'b_ada': nrm(ks[5], (L, 6 * D_MODEL), 0.02),
        'w_in': nrm(ks[6], (L, D_MODEL, P_TOTAL), D_MODEL ** -0.5),
        'gm_ln_g': 1.0 + nrm(ks[7], (L, GM_W), 0.02),
        'gm_ln_b': nrm(ks[8], (L, GM_W), 0.02),
        'gm_ws': nrm(ks[9], (L, GM_GROUPS, GM_CHUNK, GM_CHUNK), GM_CHUNK ** -0.5),
        'gm_bs': 1.0 + nrm(ks[10], (L, GM_GROUPS, GM_CHUNK), 0.1),
        'ml_conv_w': nrm(ks[11], (L, CONV_K, 2 * ML_W), CONV_K ** -0.5),
        'ml_conv_b': nrm(ks[14], (L, 2 * ML_W), 0.02),
        'ml_gate_b': ml_gate_b,
        'ml_norm_g': 1.0 + nrm(ks[15], (L, ML_W), 0.02),
        'nsa_pe_k': nrm(ks[16], (L, CMP_BLOCK, NSA_DH), 0.1),
        'nsa_pe_v': nrm(ks[17], (L, CMP_BLOCK, NSA_DH), 0.1),
        'nsa_phi_k1': nrm(ks[18], (L, CMP_BLOCK * NSA_DH, NSA_DH), (CMP_BLOCK * NSA_DH) ** -0.5),
        'nsa_phi_k2': nrm(ks[19], (L, NSA_DH, NSA_DH), NSA_DH ** -0.5),
        'nsa_phi_v1': nrm(ks[20], (L, CMP_BLOCK * NSA_DH, NSA_DH), (CMP_BLOCK * NSA_DH) ** -0.5),
        'nsa_phi_v2': nrm(ks[21], (L, NSA_DH, NSA_DH), NSA_DH ** -0.5),
        'w_up_a': nrm(ks[22], (L, GM_W, D_MODEL), GM_W ** -0.5),
        'w_up_b': nrm(ks[23], (L, ML_W, D_MODEL), ML_W ** -0.5),
        'w_up_c': nrm(ks[24], (L, NSA_W, D_MODEL), NSA_W ** -0.5),
        'w_out': nrm(ks[25], (L, D_MODEL, D_MODEL), D_MODEL ** -0.5),
        'w_mlp1': nrm(ks[26], (L, D_MODEL, D_FF), D_MODEL ** -0.5),
        'w_mlp2': nrm(ks[27], (L, D_FF, D_MODEL), D_FF ** -0.5),
        'g_final': 1.0 + nrm(ks[28], (D_MODEL,), 0.02),
    }

def second_block(x, c, g_norm1, g_norm2, w_ada, b_ada, w_in, gm_ln_g, gm_ln_b, gm_ws, gm_bs,
              ml_conv_w, ml_conv_b, ml_gate_b, ml_norm_g, nsa_pe_k, nsa_pe_v, nsa_phi_k1, nsa_phi_k2,
              nsa_phi_v1, nsa_phi_v2, w_up_a, w_up_b, w_up_c, w_out, w_mlp1, w_mlp2, g_final):
    cond = jax.nn.silu(c)
    for l in range(DEPTH_2):
        mod = (cond @ w_ada[l] + b_ada[l])[:, None, :]
        sh1, sc1, gt1, sh2, sc2, gt2 = jnp.split(mod, 6, axis=-1)
        h = rms_norm(x, g_norm1[l]) * (1.0 + sc1) + sh1
        x = x + gt1 * hybrid_mixer(h, w_in[l], gm_ln_g[l], gm_ln_b[l], gm_ws[l], gm_bs[l],
                                   ml_conv_w[l], ml_conv_b[l], ml_gate_b[l], ml_norm_g[l],
                                   nsa_pe_k[l], nsa_pe_v[l], nsa_phi_k1[l], nsa_phi_k2[l],
                                   nsa_phi_v1[l], nsa_phi_v2[l], w_up_a[l], w_up_b[l], w_up_c[l], w_out[l])
        h = rms_norm(x, g_norm2[l]) * (1.0 + sc2) + sh2
        x = x + gt2 * (jnp.square(jax.nn.relu(h @ w_mlp1[l])) @ w_mlp2[l])
    return rms_norm(x, g_final)


_first_inputs_2 = second_inputs


def second_inputs(seed=0):
    import zlib

    import numpy as np

    out = dict(_first_inputs_2(seed))
    spreads = {}
    factors = {'g_norm1': 8.0,
     'g_norm2': 24.037,
     'gm_ln_g': 38.318,
     'gm_ln_b': 39.729,
     'gm_bs': 7.936,
     'ml_conv_b': 64.0,
     'ml_norm_g': 64.0,
     'nsa_pe_k': 24.976,
     'nsa_pe_v': 53.439,
     'nsa_phi_k1': 8.0,
     'nsa_phi_k2': 8.0,
     'g_final': 7.547,
     'ml_conv_w': 6.663}
    for name, (base, spread) in spreads.items():
        noise = np.random.default_rng([zlib.crc32(name.encode()), seed]).standard_normal(out[name].shape)
        drawn = base * np.exp(spread * noise) if base else spread * noise
        out[name] = jnp.asarray(drawn.astype(out[name].dtype))
    for name, factor in factors.items():
        out[name] = (out[name] * factor).astype(out[name].dtype)
    return out


_narrow_inputs_2 = second_inputs


def second_inputs(seed=0):

    out = dict(_narrow_inputs_2(seed))
    wider = {'g_norm2': 3.05,
     'gm_ln_g': 3.23,
     'gm_ln_b': 3.2,
     'ml_conv_b': 12.0,
     'ml_norm_g': 8.74,
     'nsa_pe_k': 4.58,
     'nsa_pe_v': 3.14,
     'g_final': 3.14}
    for name, times in wider.items():
        mean = out[name].mean()
        out[name] = (mean + times * (out[name] - mean)).astype(out[name].dtype)
    return out


DEPTH_3 = 1

GDN_HEADS = 8
GDN_HEAD_DIM = 64
GDN_WIDTH = GDN_HEADS * GDN_HEAD_DIM
GDN_CONV = 4
GDN_CHUNK = 64
RWKV_HEADS = 8
RWKV_HEAD_DIM = 64
RWKV_WIDTH = RWKV_HEADS * RWKV_HEAD_DIM
DECAY_LORA = 64
ICLR_LORA = 64
GATE_LORA = 160
RWKV_COLS = 3 * RWKV_WIDTH + DECAY_LORA + ICLR_LORA + GATE_LORA
IN_SIZES = (3 * GDN_WIDTH, GDN_WIDTH, GDN_HEADS, GDN_HEADS, RWKV_COLS, D_MODEL, D_MODEL)
D_IN = 3 * GDN_WIDTH + GDN_WIDTH + 2 * GDN_HEADS + RWKV_COLS + 2 * D_MODEL
D_FF_3 = 2816
FFN_CONV = 3
NORM_EPS = 1e-6
LNX_EPS = 64e-5


def rms_norm_3(x, w, eps=NORM_EPS):
    xf = x.astype(jnp.float32)
    y = xf * lax.rsqrt(jnp.mean(xf * xf, axis=-1, keepdims=True) + eps)
    return (y * w.astype(jnp.float32)).astype(x.dtype)

def l2_normalize(x, eps=1e-6):
    xf = x.astype(jnp.float32)
    return xf * lax.rsqrt(jnp.sum(xf * xf, axis=-1, keepdims=True) + eps)

def split_cols(p, sizes):
    out, start = [], 0
    for s in sizes:
        out.append(p[..., start:start + s])
        start += s
    return out

def token_shift(p):
    return jnp.pad(p, ((0, 0), (1, 0), (0, 0)))[:, :-1]

def causal_depthwise_conv(x, w):
    k = w.shape[0]
    return lax.conv_general_dilated(
        x, w[:, None, :].astype(x.dtype), window_strides=(1,), padding=((k - 1, 0),),
        dimension_numbers=('NWC', 'WIO', 'NWC'), feature_group_count=x.shape[-1])

def chunk_gated_delta_rule(q, k, v, g, beta):
    B, T, H, dk = q.shape
    dv = v.shape[-1]
    C = GDN_CHUNK
    n = T // C
    to_chunks = lambda t: t.reshape(B, n, C, H, -1).transpose(0, 3, 1, 2, 4)
    q, k, v = to_chunks(q), to_chunks(k), to_chunks(v)
    g = g.reshape(B, n, C, H).transpose(0, 3, 1, 2)
    beta = beta.reshape(B, n, C, H).transpose(0, 3, 1, 2)
    g_cum = jnp.cumsum(g, axis=-1)
    causal = jnp.tril(jnp.ones((C, C), dtype=bool))
    strict = jnp.tril(jnp.ones((C, C), dtype=bool), -1)
    diff = g_cum[..., :, None] - g_cum[..., None, :]
    decay = jnp.where(causal, jnp.exp(jnp.where(causal, diff, 0.0)), 0.0)
    k_beta = k * beta[..., None]
    v_beta = v * beta[..., None]
    lower = jnp.where(strict, jnp.einsum('bhncd,bhnsd->bhncs', k_beta, k) * decay, 0.0)
    eye = jnp.eye(C, dtype=q.dtype)
    t_mat = lax.linalg.triangular_solve(lower + eye, jnp.broadcast_to(eye, lower.shape),
                                        left_side=True, lower=True, unit_diagonal=True)
    u = jnp.matmul(t_mat, v_beta)
    w = jnp.matmul(t_mat, k_beta * jnp.exp(g_cum)[..., None])
    attn = jnp.where(causal, jnp.einsum('bhncd,bhnsd->bhncs', q, k) * decay, 0.0)

    def step(S, inp):
        q_i, k_i, u_i, w_i, a_i, gc_i = inp
        v_new = u_i - jnp.matmul(w_i, S)
        o_i = jnp.matmul(q_i * jnp.exp(gc_i)[..., None], S) + jnp.matmul(a_i, v_new)
        g_last = gc_i[..., -1]
        k_dec = k_i * jnp.exp(g_last[..., None] - gc_i)[..., None]
        S = S * jnp.exp(g_last)[..., None, None] + jnp.einsum('bhcd,bhce->bhde', k_dec, v_new)
        return S, o_i

    mv = lambda t: jnp.moveaxis(t, 2, 0)
    S0 = jnp.zeros((B, H, dk, dv), dtype=q.dtype)
    _, o = lax.scan(step, S0, (mv(q), mv(k), mv(u), mv(w), mv(attn), mv(g_cum)))
    return o.transpose(1, 0, 3, 2, 4).reshape(B, T, H, dv)

def gated_deltanet(qkv, z, b_logit, a_logit, conv_w, a_log, dt_bias, onorm_w):
    B, T, _ = qkv.shape
    qkv = jax.nn.silu(causal_depthwise_conv(qkv, conv_w)).astype(jnp.float32)
    q, k, v = jnp.split(qkv, 3, axis=-1)
    heads = lambda t: t.reshape(B, T, GDN_HEADS, GDN_HEAD_DIM)
    q = l2_normalize(heads(q)) * (GDN_HEAD_DIM ** -0.5)
    k = l2_normalize(heads(k))
    v = heads(v)
    beta = jax.nn.sigmoid(b_logit.astype(jnp.float32))
    g = -jnp.exp(a_log.astype(jnp.float32)) * jax.nn.softplus(
        a_logit.astype(jnp.float32) + dt_bias.astype(jnp.float32))
    o = chunk_gated_delta_rule(q, k, v, g, beta)
    o = rms_norm_3(o, onorm_w) * jax.nn.silu(heads(z).astype(jnp.float32))
    return o.reshape(B, T, GDN_WIDTH)

def rwkv7_scan(r, decay, k, v, a, b):
    B, T, H, N = r.shape

    def step(S, inp):
        r_t, w_t, k_t, v_t, a_t, b_t = inp
        sa = jnp.einsum('bhvk,bhk->bhv', S, a_t)
        S = S * w_t[:, :, None, :] + sa[..., None] * b_t[:, :, None, :] + v_t[..., None] * k_t[:, :, None, :]
        return S, jnp.einsum('bhvk,bhk->bhv', S, r_t)

    tm = lambda t: jnp.moveaxis(t, 1, 0)
    S0 = jnp.zeros((B, H, N, N), dtype=jnp.float32)
    _, y = lax.scan(step, S0, (tm(r), tm(decay), tm(k), tm(v), tm(a), tm(b)))
    return jnp.moveaxis(y, 0, 1)

def rwkv7_time_mix(pb, mu, w0, w2, a0, a2, g2, k_k, k_a, r_k, lnx_w, lnx_b):
    f32 = lambda t: t.astype(jnp.float32)
    B, T, _ = pb.shape
    pb = f32(pb)
    pb = pb + (token_shift(pb) - pb) * f32(mu)
    r, k, v, w_lo, a_lo, g_lo = split_cols(
        pb, (RWKV_WIDTH, RWKV_WIDTH, RWKV_WIDTH, DECAY_LORA, ICLR_LORA, GATE_LORA))
    w = -jax.nn.softplus(-(f32(w0) + jnp.tanh(w_lo) @ f32(w2))) - 0.5
    decay = jnp.exp(-jnp.exp(w))
    a = jax.nn.sigmoid(f32(a0) + a_lo @ f32(a2))
    g = jax.nn.sigmoid(g_lo) @ f32(g2)
    heads = lambda t: t.reshape(B, T, RWKV_HEADS, RWKV_HEAD_DIM)
    kk = l2_normalize(heads(k * f32(k_k)))
    k = k * (1.0 + (a - 1.0) * f32(k_a))
    r, k, v, a, decay = heads(r), heads(k), heads(v), heads(a), heads(decay)
    y = rwkv7_scan(r, decay, k, v, -kk, kk * a)
    mean = jnp.mean(y, axis=-1, keepdims=True)
    var = jnp.mean(jnp.square(y - mean), axis=-1, keepdims=True)
    y = ((y - mean) * lax.rsqrt(var + LNX_EPS)).reshape(B, T, RWKV_WIDTH) * f32(lnx_w) + f32(lnx_b)
    bonus = jnp.sum(r * k * f32(r_k), axis=-1, keepdims=True) * v
    return (y + bonus.reshape(B, T, RWKV_WIDTH)) * g

def conv_glu(h, w_in, conv_w, w_out):
    gate, up = jnp.split(h @ w_in, 2, axis=-1)
    gate = causal_depthwise_conv(gate, conv_w)
    return (jax.nn.silu(gate) * up) @ w_out

def third_inputs(seed: int = 0) -> dict:
    key = jax.random.key(seed)
    ks = iter(jax.random.split(key, 40))
    nrm = lambda shape, scale: jax.random.normal(next(ks), shape, jnp.float32) * scale
    uni = lambda shape, lo, hi: jax.random.uniform(next(ks), shape, jnp.float32, minval=lo, maxval=hi)
    L = DEPTH_3
    x = nrm((BATCH, SEQ, D_MODEL), 1.0)
    c = nrm((BATCH, D_MODEL), 1.0)
    w_ada = nrm((L, D_MODEL, 6 * D_MODEL), D_MODEL ** -0.5)
    b_ada = nrm((L, 6 * D_MODEL), 0.02)
    norm1_w = 1.0 + nrm((L, D_MODEL), 0.02)
    w_in = nrm((L, D_MODEL, D_IN), D_MODEL ** -0.5)
    conv_gdn = nrm((L, GDN_CONV, 3 * GDN_WIDTH), GDN_CONV ** -0.5)
    a_log = jnp.log(uni((L, GDN_HEADS), 1.0, 16.0))
    dt = jnp.exp(uni((L, GDN_HEADS), math.log(1e-3), math.log(1e-1)))
    dt_bias = dt + jnp.log(-jnp.expm1(-dt))
    onorm_gdn = 1.0 + nrm((L, GDN_HEAD_DIM), 0.02)
    w_branch_gdn = nrm((L, GDN_WIDTH, D_MODEL), GDN_WIDTH ** -0.5)
    mu_rwkv = uni((L, RWKV_COLS), 0.0, 1.0)
    w0 = uni((L, RWKV_WIDTH), -6.5, -1.5)
    w2 = nrm((L, DECAY_LORA, RWKV_WIDTH), 0.5 * DECAY_LORA ** -0.5)
    a0 = nrm((L, RWKV_WIDTH), 0.1)
    a2 = nrm((L, ICLR_LORA, RWKV_WIDTH), 0.5 * ICLR_LORA ** -0.5)
    g2 = nrm((L, GATE_LORA, RWKV_WIDTH), GATE_LORA ** -0.5)
    k_k = 0.85 + nrm((L, RWKV_WIDTH), 0.02)
    k_a = 1.0 + nrm((L, RWKV_WIDTH), 0.02)
    r_k = nrm((L, RWKV_HEADS, RWKV_HEAD_DIM), 0.1)
    lnx_w = 1.0 + nrm((L, RWKV_WIDTH), 0.02)
    lnx_b = nrm((L, RWKV_WIDTH), 0.02)
    w_branch_rwkv = nrm((L, RWKV_WIDTH, D_MODEL), RWKV_WIDTH ** -0.5)
    w_out = nrm((L, D_MODEL, D_MODEL), D_MODEL ** -0.5)
    norm2_w = 1.0 + nrm((L, D_MODEL), 0.02)
    w_ffn_in = nrm((L, D_MODEL, 2 * D_FF_3), D_MODEL ** -0.5)
    conv_ffn = nrm((L, FFN_CONV, D_FF_3), FFN_CONV ** -0.5)
    w_ffn_out = nrm((L, D_FF_3, D_MODEL), D_FF_3 ** -0.5)
    norm_f_w = 1.0 + nrm((D_MODEL,), 0.02)
    return {"x": x, "c": c, "w_ada": w_ada, "b_ada": b_ada, "norm1_w": norm1_w, "w_in": w_in,
            "conv_gdn": conv_gdn, "a_log": a_log, "dt_bias": dt_bias, "onorm_gdn": onorm_gdn,
            "w_branch_gdn": w_branch_gdn, "mu_rwkv": mu_rwkv, "w0": w0, "w2": w2, "a0": a0, "a2": a2,
            "g2": g2, "k_k": k_k, "k_a": k_a, "r_k": r_k, "lnx_w": lnx_w, "lnx_b": lnx_b,
            "w_branch_rwkv": w_branch_rwkv, "w_out": w_out, "norm2_w": norm2_w, "w_ffn_in": w_ffn_in,
            "conv_ffn": conv_ffn, "w_ffn_out": w_ffn_out, "norm_f_w": norm_f_w}

def third_block(x, c, w_ada, b_ada, norm1_w, w_in, conv_gdn, a_log, dt_bias, onorm_gdn, w_branch_gdn,
              mu_rwkv, w0, w2, a0, a2, g2, k_k, k_a, r_k, lnx_w, lnx_b, w_branch_rwkv, w_out,
              norm2_w, w_ffn_in, conv_ffn, w_ffn_out, norm_f_w):
    cond = jax.nn.silu(c)
    for i in range(DEPTH_3):
        mod = cond @ w_ada[i] + b_ada[i]
        shift1, scale1, gate1, shift2, scale2, gate2 = jnp.split(mod[:, None, :], 6, axis=-1)
        h = rms_norm_3(x, norm1_w[i]) * (1.0 + scale1) + shift1
        p = h @ w_in[i]
        qkv_a, z_a, b_a, a_a, p_b, gl_a, gl_b = split_cols(p, IN_SIZES)
        y_a = gated_deltanet(qkv_a, z_a, b_a, a_a, conv_gdn[i], a_log[i], dt_bias[i], onorm_gdn[i])
        y_b = rwkv7_time_mix(p_b, mu_rwkv[i], w0[i], w2[i], a0[i], a2[i], g2[i], k_k[i], k_a[i],
                             r_k[i], lnx_w[i], lnx_b[i])
        y_a = y_a.astype(x.dtype) @ w_branch_gdn[i]
        y_b = y_b.astype(x.dtype) @ w_branch_rwkv[i]
        merged = jax.nn.sigmoid(gl_a) * y_a + jax.nn.sigmoid(gl_b) * y_b
        x = x + gate1 * (merged @ w_out[i])
        h = rms_norm_3(x, norm2_w[i]) * (1.0 + scale2) + shift2
        x = x + gate2 * conv_glu(h, w_ffn_in[i], conv_ffn[i], w_ffn_out[i])
    return rms_norm_3(x, norm_f_w)


_first_inputs_3 = third_inputs


def third_inputs(seed=0):
    import zlib

    import numpy as np

    out = dict(_first_inputs_3(seed))
    spreads = {}
    factors = {'norm1_w': 4.663,
     'onorm_gdn': 47.007,
     'w2': 14.797,
     'a0': 7.089,
     'k_k': 32.912,
     'k_a': 4.245,
     'lnx_w': 64.0,
     'lnx_b': 64.0,
     'norm2_w': 27.922,
     'norm_f_w': 7.446}
    for name, (base, spread) in spreads.items():
        noise = np.random.default_rng([zlib.crc32(name.encode()), seed]).standard_normal(out[name].shape)
        drawn = base * np.exp(spread * noise) if base else spread * noise
        out[name] = __import__('jax').numpy.asarray(drawn.astype(out[name].dtype))
    for name, factor in factors.items():
        out[name] = (out[name] * factor).astype(out[name].dtype)
    return out


_narrow_inputs_3 = third_inputs


def third_inputs(seed=0):

    out = dict(_narrow_inputs_3(seed))
    wider = {'k_k': 12.0, 'k_a': 3.66, 'lnx_w': 11.56, 'lnx_b': 11.86, 'norm_f_w': 3.02}
    for name, times in wider.items():
        mean = out[name].mean()
        out[name] = (mean + times * (out[name] - mean)).astype(out[name].dtype)
    return out


def setup_inputs(seed=0):
    out = dict(first_inputs(seed))
    for name, value in second_inputs(seed + 1).items():
        if name != "x":
            out[name + "_2"] = value
    for name, value in third_inputs(seed + 2).items():
        if name != "x":
            out[name + "_3"] = value
    return out


def reference(
    x, c, ctx, c_ctx, norm_g, ada_w, ada_b, hgrn_w_in, hgrn_lb_logits, hgrn_norm_g, hgrn_w_out,
    conv_w_in, conv_b_in, conv_dw, conv_dw_b, conv_ln_g, conv_ln_b, conv_w_out, conv_b_out,
    final_norm_g, c_2, g_norm1_2, g_norm2_2, w_ada_2, b_ada_2, w_in_2, gm_ln_g_2, gm_ln_b_2,
    gm_ws_2, gm_bs_2, ml_conv_w_2, ml_conv_b_2, ml_gate_b_2, ml_norm_g_2, nsa_pe_k_2,
    nsa_pe_v_2, nsa_phi_k1_2, nsa_phi_k2_2, nsa_phi_v1_2, nsa_phi_v2_2, w_up_a_2, w_up_b_2,
    w_up_c_2, w_out_2, w_mlp1_2, w_mlp2_2, g_final_2, c_3, w_ada_3, b_ada_3, norm1_w_3, w_in_3,
    conv_gdn_3, a_log_3, dt_bias_3, onorm_gdn_3, w_branch_gdn_3, mu_rwkv_3, w0_3, w2_3, a0_3,
    a2_3, g2_3, k_k_3, k_a_3, r_k_3, lnx_w_3, lnx_b_3, w_branch_rwkv_3, w_out_3, norm2_w_3,
    w_ffn_in_3, conv_ffn_3, w_ffn_out_3, norm_f_w_3,
):
    x = first_block(
        x, c, ctx, c_ctx, norm_g, ada_w, ada_b, hgrn_w_in, hgrn_lb_logits, hgrn_norm_g,
        hgrn_w_out, conv_w_in, conv_b_in, conv_dw, conv_dw_b, conv_ln_g, conv_ln_b, conv_w_out,
        conv_b_out, final_norm_g,
    )
    x = second_block(
        x, c_2, g_norm1_2, g_norm2_2, w_ada_2, b_ada_2, w_in_2, gm_ln_g_2, gm_ln_b_2, gm_ws_2,
        gm_bs_2, ml_conv_w_2, ml_conv_b_2, ml_gate_b_2, ml_norm_g_2, nsa_pe_k_2, nsa_pe_v_2,
        nsa_phi_k1_2, nsa_phi_k2_2, nsa_phi_v1_2, nsa_phi_v2_2, w_up_a_2, w_up_b_2, w_up_c_2,
        w_out_2, w_mlp1_2, w_mlp2_2, g_final_2,
    )
    return third_block(
        x, c_3, w_ada_3, b_ada_3, norm1_w_3, w_in_3, conv_gdn_3, a_log_3, dt_bias_3,
        onorm_gdn_3, w_branch_gdn_3, mu_rwkv_3, w0_3, w2_3, a0_3, a2_3, g2_3, k_k_3, k_a_3,
        r_k_3, lnx_w_3, lnx_b_3, w_branch_rwkv_3, w_out_3, norm2_w_3, w_ffn_in_3, conv_ffn_3,
        w_ffn_out_3, norm_f_w_3,
    )


_drawn_inputs = setup_inputs


def setup_inputs(seed=0):
    import zlib

    import numpy as np

    out = dict(_drawn_inputs(seed))
    spreads = {}
    factors = {}
    for name, (base, spread) in spreads.items():
        noise = np.random.default_rng([zlib.crc32(name.encode()), seed]).standard_normal(out[name].shape)
        drawn = base * np.exp(spread * noise) if base else spread * noise
        out[name] = jnp.asarray(drawn.astype(out[name].dtype))
    for name, factor in factors.items():
        out[name] = (out[name] * factor).astype(out[name].dtype)
    return out
```

```python
import numpy as np
import concourse.bass as bass
from concourse import mybir
from contextlib import ExitStack

F32 = mybir.dt.float32
F32R = mybir.dt.float32r
U32 = mybir.dt.uint32
ALU = mybir.AluOpType
ACT = mybir.ActivationFunctionType
AX = mybir.AxisListType
P = 128
DM = 1024
KD = DM // P
T = 512
TC = 256
EPS = 1e-6
LOG_EXP_SET = "natural_log_exp_and_others"


def flat_rows(ap, n):
    names = "abcd"[:len(ap.shape)]
    v = ap.rearrange(f"{' '.join(names)} -> ({' '.join(names)})") if len(ap.shape) > 1 else ap
    return v[0:n * P].rearrange("(r p) -> r p", p=P)


class Kit:

    def __init__(self, nc, ctx, inp):
        self.nc, self.ctx, self.inp = nc, ctx, inp
        self.pools = [[ctx.enter_context(nc.semaphore(f"phase{k}_sem{n}")) for n in range(32)] for k in (0, 1)]
        self.turn = 0
        self.used = {}
        self.phases = 0

    def unique(self, name):
        self.used[name] = self.used.get(name, 0) + 1
        return name if self.used[name] == 1 else f"{name}_{self.used[name]}"

    def sb(self, stack, name, shape, dt=F32):
        return stack.enter_context(self.nc.sbuf_tensor(self.unique(name), shape, dt))

    def psum_banks(self, stack, tag):
        return [stack.enter_context(self.nc.psum_tensor(self.unique(f"{tag}_bank{i}"), [P, 512], F32)) for i in range(8)]

    def phase(self):
        mine, old = self.pools[self.turn], self.pools[1 - self.turn]
        self.turn = 1 - self.turn
        clear = old if self.phases else []
        self.phases += 1
        return list(mine), clear


def clear_old(sp, old):
    for s in old:
        sp.sem_clear(s)


def vec_rows(inp):
    x = inp
    out = [("cond", x["c"], KD), ("cond_ctx", x["c_ctx"], KD), ("cond2", x["c_2"], KD), ("cond3", x["c_3"], KD),
           ("ada_b", x["ada_b"], 48), ("ada_b2", x["b_ada_2"], 48), ("ada_b3", x["b_ada_3"], 48),
           ("norm_g", x["norm_g"], 16), ("lb", x["hgrn_lb_logits"], 32), ("hgrn_g", x["hgrn_norm_g"], 1),
           ("conv_b_in", x["conv_b_in"], 48), ("conv_dw", x["conv_dw"], 496), ("conv_dw_b", x["conv_dw_b"], 16),
           ("conv_ln_g", x["conv_ln_g"], 16), ("conv_ln_b", x["conv_ln_b"], 16), ("conv_b_out", x["conv_b_out"], 8),
           ("final_g", x["final_norm_g"], 8),
           ("g1_2", x["g_norm1_2"], 8), ("g2_2", x["g_norm2_2"], 8), ("ml_w", x["ml_conv_w_2"], 32),
           ("ml_b", x["ml_conv_b_2"], 8), ("ml_g", x["ml_norm_g_2"], 4), ("final_2", x["g_final_2"], 8),
           ("g1_3", x["norm1_w_3"], 8), ("gdn_w", x["conv_gdn_3"], 48), ("mu", x["mu_rwkv_3"], 14),
           ("w0", x["w0_3"], 4), ("a0", x["a0_3"], 4), ("k_k", x["k_k_3"], 4), ("k_a", x["k_a_3"], 4),
           ("r_k", x["r_k_3"], 4), ("lnx_w", x["lnx_w_3"], 4), ("lnx_b", x["lnx_b_3"], 4),
           ("g2_3", x["norm2_w_3"], 8), ("ffn_w", x["conv_ffn_3"], 66), ("final_3", x["norm_f_w_3"], 8)]
    return out


def constants_phase(K):
    nc, inp = K.nc, K.inp
    rows = vec_rows(inp)
    K.at, n = {}, 0
    for name, _, r in rows:
        K.at[name] = n
        n += r
    extra = n
    K.at["mu_tail"], K.at["onorm"] = extra, extra + 1
    n += 2
    tiles = -(-n // P)
    K.epsc = K.sb(K.ctx, "epsc", [P, 1])
    K.vec = K.sb(K.ctx, "vec", [P, tiles * P])
    K.ident = K.sb(K.ctx, "ident", [P, P])
    K.ones = K.sb(K.ctx, "ones", [P, P])
    K.tri = K.sb(K.ctx, "tri", [P, P])
    K.xT = K.sb(K.ctx, "xT", [P, KD, T])
    K.hT = K.sb(K.ctx, "hT", [P, KD, T])
    K.mod = K.sb(K.ctx, "mod", [P, 144, 4])
    K.cond = K.sb(K.ctx, "condT", [P, KD, 4])
    K.early = ExitStack()
    K.ctxT = K.sb(K.early, "ctxT", [P, KD, TC])
    with ExitStack() as st:
        raw = K.sb(st, "vec_raw", [P, tiles, P])
        xin = K.sb(st, "x_tok", [P, T // P, DM])
        cin = K.sb(st, "ctx_tok", [P, TC // P, DM])
        ps = K.psum_banks(st, "const")
        sems, _ = K.phase()
        loaded, zeroed, made, transposed, copied, silu, x_in = sems[:7]
        pieces = []
        for name, ap, r in rows:
            src = flat_rows(ap, r)
            a, done = K.at[name], 0
            while done < r:
                k = min(r - done, P - (a + done) % P)
                pieces.append((raw[(a + done) % P:(a + done) % P + k, (a + done) // P, :], src[done:done + k, :]))
                done += k
        mt = inp["mu_rwkv_3"].rearrange("a n -> (a n)")
        pieces.append((raw[extra % P:extra % P + 1, extra // P, 0:32], mt[14 * P:14 * P + 32].rearrange("(a n) -> a n", a=1)))
        og = inp["onorm_gdn_3"]
        for half in (0, 1):
            pieces.append((raw[(extra + 1) % P:(extra + 1) % P + 1, (extra + 1) // P, 64 * half:64 * half + 64], og[0:1, :]))
        with nc.Block() as block:
            @block.sync
            def _(sp):
                sp.dma_start(xin[:, :, :], inp["x"].rearrange("a (t p) d -> p (a t) d", p=P)).then_inc(x_in, 16)
                sp.dma_start(cin[:, :, :], inp["ctx"].rearrange("a (t p) d -> p (a t) d", p=P)).then_inc(x_in, 16)
                sp.wait_ge(zeroed, 1)
                for dst, src in pieces:
                    sp.dma_start(dst, src).then_inc(loaded, 16)

            @block.gpsimd
            def _(pool):
                pool.memset(raw[:, tiles - 1, :], 0.0).then_inc(zeroed, 1)
                pool.memset(K.ident[:, :], 0.0).then_inc(made, 1)
                pool.memset(K.ones[:, :], 1.0).then_inc(made, 1)
                pool.memset(K.epsc[:, :], EPS).then_inc(made, 1)
                pool.memset(K.tri[:, :], 1.0).then_inc(made, 1)
                pool.wait_ge(made, 4)
                pool.affine_select(out=K.tri[:, :], in_=K.tri[:, :], compare_op=ALU.is_ge, fill=0.0, base=0,
                                   pattern=[[1, P]], channel_multiplier=-1).then_inc(made, 1)
                pool.affine_select(out=K.ident[:, :], in_=K.ident[:, :], compare_op=ALU.not_equal, fill=1.0,
                                   base=0, pattern=[[-1, P]], channel_multiplier=1).then_inc(made, 1)

            @block.tensor
            def _(pe):
                pe.wait_ge(made, 6)
                pe.wait_ge(x_in, 32)
                n = 0
                for src, count in ((xin, T // P), (cin, TC // P)):
                    for k in range(KD):
                        if n >= 8:
                            pe.wait_ge(copied, n - 7)
                        for t in range(count):
                            ins = pe.transpose(ps[n % 8][:, t * P:(t + 1) * P], src[:, t, k * P:(k + 1) * P], K.ident[:, :])
                        ins.then_inc(transposed, 1)
                        n += 1
                pe.wait_ge(loaded, 16 * len(pieces))
                for g in range(0, tiles, 4):
                    pe.wait_ge(copied, n - 7)
                    for t in range(g, min(g + 4, tiles)):
                        ins = pe.transpose(ps[n % 8][:, (t - g) * P:(t - g + 1) * P], raw[:, t, :], K.ident[:, :])
                    ins.then_inc(transposed, 1)
                    n += 1

            @block.vector
            def _(dve):
                n = 0
                for dst, width in ((K.xT, T), (K.ctxT, TC)):
                    for k in range(KD):
                        dve.wait_ge(transposed, n + 1)
                        dve.tensor_copy(dst[:, k, :], ps[n % 8][:, 0:width]).then_inc(copied, 1)
                        n += 1
                for g in range(0, tiles, 4):
                    w = (min(g + 4, tiles) - g) * P
                    dve.wait_ge(transposed, n + 1)
                    dve.tensor_copy(K.vec[:, g * P:g * P + w], ps[n % 8][:, 0:w]).then_inc(copied, 1)
                    n += 1

            @block.scalar
            def _(act):
                act.wait_ge(copied, 2 * KD + -(-tiles // 4))
                for v, name in enumerate(("cond", "cond_ctx", "cond2", "cond3")):
                    a = K.at[name]
                    act.activation(K.cond[:, :, v], K.vec[:, a:a + KD], ACT.Silu).then_inc(silu, 1)


def modulation_phase(K):
    nc, inp = K.nc, K.inp
    GC = 512
    SLOTS = 3
    mats = [(inp["ada_w"][0], 6), (inp["ada_w"][1], 6), (inp["w_ada_2"][0], 12), (inp["w_ada_3"][0], 12)]
    rounds = sum(groups for _, groups in mats) // SLOTS
    bias = K.at["ada_b"]
    with ExitStack() as st:
        w = [K.sb(st, f"ada_w{i}", [P, KD, GC]) for i in range(SLOTS)]
        wh = [K.sb(st, f"ada_wh{i}", [P, KD, GC], F32R) for i in range(SLOTS)]
        wl = [K.sb(st, f"ada_wl{i}", [P, KD, GC], F32R) for i in range(SLOTS)]
        c8 = K.sb(st, "ada_cond", [P, KD, 8], F32R)
        sums = K.sb(st, "ada_sums", [8, SLOTS, GC])
        pick = K.sb(st, "ada_pick", [8, 4])
        ps = K.psum_banks(st, "ada")
        sems, old = K.phase()
        w_in = sems[0:SLOTS]
        high, low, summed, copied, turned, biased, c_high, ready = sems[SLOTS:SLOTS + 8]
        with nc.Block() as block:
            @block.sync
            def _(sp):
                clear_old(sp, old)
                done = 0
                for mat, groups in mats:
                    src = mat.rearrange("(k p) n -> p k n", p=P)
                    with sp.Fori(0, groups // SLOTS) as i:
                        for s in range(SLOTS):
                            sp.wait_ge(summed, SLOTS * i + (done + s + 1))
                            sp.dma_start(w[s][:, :, :], src[:, :, bass.ds((SLOTS * i + s) * GC, GC)]).then_inc(w_in[s], 16)
                    done += groups

            @block.tensor
            def _(pe):
                pe.sem_inc(summed, SLOTS)
                pe.wait_ge(ready, 2)
                with pe.Fori(0, rounds) as i:
                    for s in range(SLOTS):
                        pe.wait_ge(low, SLOTS * i + (s + 1))
                        for k in range(KD):
                            pe.matmul(ps[s][0:8, :], c8[:, k, :], wh[s][:, k, :], start=(k == 0), stop=False)
                            ins = pe.matmul(ps[s][0:8, :], c8[:, k, :], wl[s][:, k, :],
                                            start=False, stop=(k == KD - 1))
                        ins.then_inc(summed, 1)
                        pe.wait_ge(copied, SLOTS * i + (s + 1))
                        pe.wait_ge(biased, SLOTS * i + (s + 1))
                        for j in range(GC // P):
                            ins = pe.matmul(ps[SLOTS + s][:, 4 * j:4 * j + 4], sums[:, s, j * P:(j + 1) * P], pick[:, :],
                                            start=True, stop=True)
                        ins.then_inc(turned, 1)

            @block.scalar
            def _(act):
                act.activation(c8[:, :, 0:4], K.cond[:, :, :], ACT.Copy).then_inc(c_high, 1)

                def round_high(i, s):
                    act.wait_ge(w_in[s], 16 * i + 16)
                    act.activation(wh[s][:, :, :], w[s][:, :, :], ACT.Copy).then_inc(high, 1)

                def copy(i, s):
                    act.wait_ge(summed, SLOTS * i + (s + 1 + SLOTS))
                    act.activation(sums[:, s, :], ps[s][0:8, :], ACT.Copy).then_inc(copied, 1)

                round_high(0, 0)
                with act.Fori(0, rounds - 1) as i:
                    for s in range(SLOTS):
                        round_high(i + (s + 1) // SLOTS, (s + 1) % SLOTS)
                        copy(i, s)
                for s in range(SLOTS):
                    if s + 1 < SLOTS:
                        round_high(rounds - 1, s + 1)
                    copy(rounds - 1, s)

            @block.vector
            def _(dve):
                dve.sem_inc(biased, SLOTS)
                dve.tensor_tensor(pick[:, :], K.ident[0:8, 0:4], K.ident[0:8, 4:8], ALU.add).then_inc(ready, 1)
                dve.wait_ge(c_high, 1)
                dve.tensor_tensor(c8[:, :, 4:8], K.cond[:, :, :], c8[:, :, 0:4].bitcast(F32), ALU.subtract).then_inc(ready, 1)

                def subtract(i, s):
                    dve.wait_ge(high, SLOTS * i + (s + 1))
                    dve.tensor_tensor(wl[s][:, :, :], w[s][:, :, :], wh[s][:, :, :].bitcast(F32),
                                      ALU.subtract).then_inc(low, 1)

                def add_bias(i, s):
                    dve.wait_ge(turned, SLOTS * i + (s + 1))
                    at = 4 * (SLOTS * i + s)
                    dve.tensor_tensor(K.mod[:, bass.ds(at, 4), :],
                                      ps[SLOTS + s][:, 0:16].rearrange("p (j v) -> p j v", v=4),
                                      K.vec[:, bass.ds(at + bias, 4)].unsqueeze(2).broadcast_to((P, 4, 4)),
                                      ALU.add).then_inc(biased, 1)

                subtract(0, 0)
                with dve.Fori(0, rounds - 1) as i:
                    for s in range(SLOTS):
                        subtract(i + (s + 1) // SLOTS, (s + 1) % SLOTS)
                        add_bias(i, s)
                for s in range(SLOTS):
                    if s + 1 < SLOTS:
                        subtract(rounds - 1, s + 1)
                    add_bias(rounds - 1, s)


NH = 16
HC = 128
EW = NH * P


def norm_phase(K, jobs):
    nc = K.nc
    with ExitStack() as st:
        sq = K.sb(st, "norm_sq", [P, 2, T])
        gain = K.sb(st, "norm_gain", [P, len(jobs), KD])
        root = K.sb(st, "norm_root", [P, len(jobs), T])
        rstd = K.sb(st, "norm_rstd", [P, len(jobs), T])
        ps = K.psum_banks(st, "norm")
        sems, old = K.phase()
        squared, summed, rooted, inverted, gained, scaled, added, chain = sems[:8]
        with nc.Block() as block:
            @block.sync
            def _(sp):
                clear_old(sp, old)

            @block.scalar
            def _(act):
                n = 0
                for j, (x, dst, w, *_) in enumerate(jobs):
                    for k in range(KD):
                        if n >= 2:
                            act.wait_ge(summed, n - 1)
                        act.activation(sq[:, n % 2, 0:w], x[:, k, 0:w], ACT.Square).then_inc(squared, 1)
                        n += 1
                for j, (x, dst, w, *_) in enumerate(jobs):
                    act.wait_ge(summed, KD * (j + 1))
                    act.activation(root[:, j, 0:w], ps[j][:, 0:w], ACT.Sqrt, scale=1.0 / DM, bias=K.epsc[:, 0:1]).then_inc(rooted, 1)
                for j, (x, dst, w, g, shift, scale, v) in enumerate(jobs):
                    if shift is not None:
                        for k in range(KD):
                            act.wait_ge(scaled, KD * j + k + 1)
                            act.activation(dst[:, k, 0:w], dst[:, k, 0:w], ACT.Identity,
                                           bias=K.mod[:, shift + k, v:v + 1]).then_inc(added, 1)

            @block.tensor
            def _(pe):
                n = 0
                for j, (x, dst, w, *_) in enumerate(jobs):
                    for k in range(KD):
                        pe.wait_ge(squared, n + 1)
                        pe.matmul(ps[j][:, 0:w], K.ones[:, :], sq[:, n % 2, 0:w], start=(k == 0), stop=(k == KD - 1)).then_inc(summed, 1)
                        n += 1

            @block.vector
            def _(dve):
                for j, (x, dst, w, g, shift, scale, v) in enumerate(jobs):
                    if shift is None:
                        dve.tensor_copy(gain[:, j, :], K.vec[:, g:g + KD]).then_inc(gained, 1)
                    else:
                        dve.scalar_tensor_tensor(gain[:, j, :], K.mod[:, scale:scale + KD, v], 1.0, K.vec[:, g:g + KD],
                                                 ALU.add, ALU.mult).then_inc(gained, 1)
                dve.wait_ge(gained, len(jobs))
                for j, (x, dst, w, g, shift, scale, v) in enumerate(jobs):
                    dve.wait_ge(rooted, j + 1)
                    dve.reciprocal(rstd[:, j, 0:w], root[:, j, 0:w]).then_inc(inverted, 1)
                    dve.wait_ge(inverted, j + 1)
                    for k in range(KD):
                        dve.scalar_tensor_tensor(dst[:, k, 0:w], x[:, k, 0:w], gain[:, j, k:k + 1], rstd[:, j, 0:w],
                                                 ALU.mult, ALU.mult).then_inc(scaled, 1)


def hgrn_phase(K, hO):
    nc, inp = K.nc, K.inp
    hT, cT = K.hT, K.ctxT
    LAT = TC
    NT = TC + T
    NCH = T // HC
    TINY = 2.0 ** -62
    V, ZF, ZB, Q, G = range(5)
    COL = {Q: 0, V: EW, ZF: 2 * EW, ZB: 3 * EW, G: 4 * EW}
    wv = inp["hgrn_w_in"][0].rearrange("(k p) n -> p k n", p=P)
    LV = ((64, 0), (32, 1), (16, 2))
    with ExitStack() as st:
        W = [K.sb(st, f"hg_w{m}", [P, KD, P]) for m in range(5)]
        vt = [K.sb(st, f"hg_v{i}", [P, NT // P, P]) for i in range(2)]
        sg = [[K.sb(st, f"hg_sig{i}{d}", [P, NT]) for d in range(2)] for i in range(2)]
        qs = [K.sb(st, f"hg_q{i}", [P, T]) for i in range(2)]
        gs = [K.sb(st, f"hg_gate{i}", [P, T]) for i in range(2)]
        f1 = [K.sb(st, f"hg_f{d}", [P, NT]) for d in range(2)]
        kk = [K.sb(st, f"hg_k{d}", [P, NT]) for d in range(2)]
        cum = [K.sb(st, f"hg_cum{d}", [P, NT]) for d in range(2)]
        lev = [K.sb(st, f"hg_lev{d}", [P, 3, T]) for d in range(2)]
        dg = [K.sb(st, f"hg_diag{d}", [P, 2, T]) for d in range(2)]
        ks = [K.sb(st, f"hg_ks{d}", [P, NT]) for d in range(2)]
        dec = [K.sb(st, f"hg_dec{d}", [P, NCH]) for d in range(2)]
        kT = [K.sb(st, f"hg_kT{d}", [P, 5, P]) for d in range(2)]
        AT = [K.sb(st, f"hg_AT{d}", [P, NCH, HC]) for d in range(2)]
        S = [K.sb(st, f"hg_S{d}", [P, NCH, P]) for d in range(2)]
        mask = [K.sb(st, f"hg_mask{d}", [P, HC]) for d in range(2)]
        keep = K.sb(st, "hg_keep", [P, T])
        probe = K.sb(st, "hg_probe", [P, 1])
        ones_c = K.sb(st, "hg_ones_c", [P, TC])
        osq = K.sb(st, "hg_osq", [P, T])
        ors = K.sb(st, "hg_ors", [P, T])
        lb = K.sb(st, "hg_lb", [P, 32])
        omlb = K.sb(st, "hg_omlb", [P, 32])
        tmp = K.sb(st, "hg_tmp", [P, 32])
        tmp2 = K.sb(st, "hg_tmp2", [P, 32])
        ps = K.psum_banks(st, "hg")
        SC, TR, KV, OUT = ps[4], ps[5], ps[6], ps[7]
        sems, old = K.phase()
        w_in = sems[0:5]
        (proj, evac, set0, lb_ok, f_ok, g_ok, k_ok, cum_ok, dif_ok, rd_ok, exp_ok, prod_ok, tr_ok, trc_ok, sc_ok,
         at_ok, kv_ok, s_ok, out_ok, sq_ok, ms_ok, ln_ok, rs_ok, o1_ok, fin_ok) = sems[5:30]
        GROUPS = [(V, 0), (V, 1), (ZF, 0), (ZF, 1), (ZB, 0), (ZB, 1), (Q, 0), (G, 0)]
        NG = len(GROUPS)
        LAST_OF = {V: 2, ZF: 4, ZB: 6, Q: 7, G: 8}

        def ctx_cols(t):
            return t[:, 0:TC]

        def lat_cols(t):
            return t[:, LAT:NT]

        with nc.Block() as block:
            @block.sync
            def _(sp):
                clear_old(sp, old)

                def load(h, first, shift=0):
                    at = h * P if first else sp.snap(h * P)
                    for m in (V, ZF, ZB, Q, G):
                        if not first:
                            sp.wait_ge(proj, NG * h + LAST_OF[m])
                        sp.dma_start(W[m][:, :, :], wv[:, :, bass.ds(at + (COL[m] + shift), P)]).then_inc(w_in[m], 16)
                load(0, True)
                with sp.Fori(0, NH - 1) as before:
                    load(before, False, P)

            @block.gpsimd
            def _(pool):
                for d in range(2):
                    pool.memset(mask[d][:, :], 1.0).then_inc(set0, 1)
                    pool.memset(AT[d][:, :, :], 0.0).then_inc(set0, 1)
                pool.memset(keep[:, :], 1.0).then_inc(set0, 1)
                pool.wait_ge(set0, 5)
                pool.memset(keep[:, 0:T:HC], 0.0).then_inc(set0, 1)
                pool.affine_select(out=mask[0][:, :], in_=mask[0][:, :], compare_op=ALU.is_ge, fill=0.0, base=0,
                                   pattern=[[1, HC]], channel_multiplier=-1).then_inc(set0, 1)
                pool.affine_select(out=mask[1][:, :], in_=mask[1][:, :], compare_op=ALU.is_ge, fill=0.0, base=0,
                                   pattern=[[-1, HC]], channel_multiplier=1).then_inc(set0, 1)

            @block.tensor
            def _(pe):
                def project(h, p, first=False):
                    for n, (m, c) in enumerate(GROUPS):
                        if c == 0:
                            pe.wait_ge(w_in[m], 16 * h + 16)
                        if n >= 4 or not first:
                            pe.wait_ge(evac, NG * h + (n - 3))
                        src, w = (cT, TC) if c else (hT, T)
                        bank = ps[n % 4]
                        if m == V:
                            for t in range(w // P):
                                for k in range(KD):
                                    ins = pe.matmul(bank[:, t * P:(t + 1) * P], src[:, k, t * P:(t + 1) * P], W[m][:, k, :],
                                                    start=(k == 0), stop=(k == KD - 1))
                        else:
                            for k in range(KD):
                                ins = pe.matmul(bank[:, 0:w], W[m][:, k, :], src[:, k, 0:w],
                                                start=(k == 0), stop=(k == KD - 1))
                        ins.then_inc(proj, 1)

                def scores(d):
                    lv = lev[d]
                    for c in range(NCH):
                        a = c * HC
                        ins = pe.matmul(SC[:, a:a + HC], dg[d][:, 1, a:a + HC], dg[d][:, 0, a:a + HC], start=True, stop=True)
                        for half, li in reversed(LV):
                            for b in range(0, HC, 2 * half):
                                if d == 0 or half > 16:
                                    s0, t0 = (b, b + half) if d == 0 else (b + half, b)
                                    ins = pe.matmul(SC[s0:s0 + half, a + t0:a + t0 + half], lv[:, li, a + s0:a + s0 + half],
                                                    lv[:, li, a + t0:a + t0 + half], start=True, stop=True)
                                else:
                                    pe.matmul(SC[b:b + 32, a + b:a + b + 16], lv[:, li, a + b:a + b + 32],
                                              lv[:, li, a + b:a + b + 16], start=True, stop=True)
                                    ins = pe.matmul(SC[b:b + 16, a + b:a + b + 16], dg[d][:, 1, a + b:a + b + 16],
                                                    dg[d][:, 0, a + b:a + b + 16], start=True, stop=True)
                    ins.then_inc(sc_ok, 1)

                def recur(h, p, very_first=False):
                    for d in range(2):
                        first = 0 if d == 0 else 1
                        pe.wait_ge(prod_ok, 2 * h + (d + 1))
                        if d == 1 or not very_first:
                            pe.wait_ge(s_ok, 8 * h + 4 * d)
                        for n in range(3):
                            a = LAT + (first + n) * HC
                            pe.transpose(TR[:, n * P:(n + 1) * P], ks[d][:, a:a + HC], K.ident[:, :])
                        for n in range(2):
                            ins = pe.transpose(KV[:, n * P:(n + 1) * P], ks[d][:, n * P:(n + 1) * P], K.ident[:, :])
                        ins.then_inc(tr_ok, 1)
                        if d == 1:
                            pe.wait_ge(at_ok, 2 * h + 1)
                        elif not very_first:
                            pe.wait_ge(ln_ok, h)
                        scores(d)
                        pe.wait_ge(trc_ok, 4 * h + (2 * d + 2))
                        for n in range(3):
                            pe.matmul(TR[:, n * P:(n + 1) * P], kT[d][:, n, :], vt[p][:, 2 + first + n, :], start=True, stop=True)
                        for n in range(2):
                            ins = pe.matmul(KV[:, 0:P], kT[d][:, 3 + n, :], vt[p][:, n, :], start=(n == 0), stop=(n == 1))
                        ins.then_inc(kv_ok, 1)
                        pe.wait_ge(at_ok, 2 * h + (d + 1))
                        for c in range(NCH):
                            pe.matmul(OUT[:, c * HC:(c + 1) * HC], vt[p][:, 2 + c, :], AT[d][:, c, :],
                                      start=(d == 0 and c == 0), stop=False, skip_group_check=True)
                        for n in range(NCH):
                            c = n if d == 0 else NCH - 1 - n
                            pe.wait_ge(s_ok, 8 * h + (4 * d + n + 1))
                            ins = pe.matmul(OUT[:, c * HC:(c + 1) * HC], S[d][:, c, :], cum[d][:, LAT + c * HC:LAT + (c + 1) * HC],
                                            start=False, stop=(d == 1), skip_group_check=True)
                    ins.then_inc(out_ok, 1)
                    pe.wait_ge(sq_ok, h + 1)
                    pe.matmul(SC[:, :], K.ones[:, :], osq[:, :], start=True, stop=True).then_inc(ms_ok, 1)

                project(0, 0, True)
                project(1, 1)
                recur(0, 0, True)
                with pe.Fori(1, NH // 2) as j:
                    project(2 * j, 0)
                    recur(2 * j - 1, 1)
                    project(2 * j + 1, 1)
                    recur(2 * j, 0)
                recur(NH - 1, 1)

            @block.scalar
            def _(act):
                act.wait_ge(f_ok, 1)
                act.activation(tmp2[:, :], tmp[:, :], ACT.Exp).then_inc(g_ok, 1)

                def evacuate(h, p, groups):
                    for n in groups:
                        m, c = GROUPS[n]
                        act.wait_ge(proj, NG * h + (n + 1))
                        bank = ps[n % 4]
                        if m == V:
                            a, w = (0, 2) if c else (2, 4)
                            act.activation(vt[p][:, a:a + w, :], bank[:, 0:w * P].rearrange("q (t v) -> q t v", v=P), ACT.Copy).then_inc(evac, 1)
                        elif m in (ZF, ZB):
                            s = sg[p][m - ZF]
                            act.activation(ctx_cols(s) if c else lat_cols(s), bank[:, 0:TC if c else T], ACT.Sigmoid).then_inc(evac, 1)
                        else:
                            act.activation((qs if m == Q else gs)[p][:, :], bank[:, :], ACT.Silu).then_inc(evac, 1)

                def logs(h):
                    act.preload_act_table_set(LOG_EXP_SET)
                    for d in range(2):
                        act.wait_ge(f_ok, 2 * h + (d + 3))
                        act.activation(cum[d][:, :], f1[d][:, :], ACT.Ln, bias=lb[:, bass.ds(h + NH * d, 1)]).then_inc(g_ok, 1)

                def exps(h, d):
                    act.wait_ge(dif_ok, 2 * h + (d + 1))
                    for half, li in LV:
                        v = lev[d][:, li, :].rearrange("q (b s t) -> q b s t", s=2, t=half)
                        for s in range(2):
                            act.activation(v[:, :, s, :], v[:, :, s, :], ACT.Exp, scale=1.0 if s == 1 - d else -1.0)
                    act.activation(dg[d][:, 1, :], dg[d][:, 0, :], ACT.Exp, scale=-1.0)
                    act.activation(ks[d][:, :], ks[d][:, :], ACT.Exp)
                    act.activation(dec[d][:, :], cum[d][:, LAT + (HC - 1 if d == 0 else 0):NT:HC], ACT.Exp).then_inc(rd_ok, 1)
                    act.wait_ge(rd_ok, 2 * h + (d + 1))
                    act.activation(dg[d][:, 0, :], dg[d][:, 0, :], ACT.Exp)
                    act.activation(lat_cols(cum[d]), lat_cols(cum[d]), ACT.Exp).then_inc(exp_ok, 1)

                def recur(h):
                    for d in range(2):
                        act.wait_ge(tr_ok, 2 * h + (d + 1))
                        act.activation(kT[d][:, 0:3, :], TR[:, 0:3 * P].rearrange("q (n k) -> q n k", k=P), ACT.Copy).then_inc(trc_ok, 1)
                        act.activation(kT[d][:, 3:5, :], KV[:, 0:2 * P].rearrange("q (n k) -> q n k", k=P), ACT.Copy).then_inc(trc_ok, 1)
                    act.wait_ge(out_ok, h + 1)
                    act.activation(osq[:, :], OUT[:, :], ACT.Square).then_inc(sq_ok, 1)
                    act.preload_act_table_set(LOG_EXP_SET)
                    act.wait_ge(ms_ok, h + 1)
                    act.activation(ors[:, :], SC[:, :], ACT.Ln, scale=1.0 / P, bias=K.epsc[:, 0:1]).then_inc(ln_ok, 1)
                    act.wait_ge(ln_ok, h + 1)
                    act.activation(ors[:, :], ors[:, :], ACT.Exp, scale=-0.5).then_inc(rs_ok, 1)

                def step(h, p):
                    logs(h - 1)
                    exps(h - 1, 0)
                    evacuate(h, p, range(0, 2))
                    exps(h - 1, 1)
                    evacuate(h, p, range(2, NG))
                    recur(h - 1)

                evacuate(0, 0, range(NG))
                step(1, 1)
                with act.Fori(1, NH // 2) as j:
                    step(2 * j, 0)
                    step(2 * j + 1, 1)
                logs(NH - 1)
                exps(NH - 1, 0)
                exps(NH - 1, 1)
                recur(NH - 1)

            @block.vector
            def _(dve):
                a = K.at["lb"]
                x = K.vec[:, a:a + 32]
                dve.tensor_tensor(tmp[:, :], x, x, ALU.subtract).then_inc(f_ok, 1)
                dve.wait_ge(g_ok, 1)
                dve.reciprocal(lb[:, :], tmp2[:, :]).then_inc(lb_ok, 1)
                dve.wait_ge(lb_ok, 1)
                dve.tensor_tensor(tmp[:, :], tmp2[:, :], lb[:, :], ALU.mult).then_inc(lb_ok, 1)
                dve.wait_ge(lb_ok, 2)
                dve.tensor_tensor(lb[:, :], tmp[:, :], tmp[:, :], ALU.subtract).then_inc(lb_ok, 1)
                dve.wait_ge(lb_ok, 3)
                dve.tensor_scalar(omlb[:, :], lb[:, :], -1.0, 1.0, ALU.mult, ALU.add).then_inc(lb_ok, 1)
                dve.memset(ones_c[:, :], 1.0).then_inc(f_ok, 1)
                dve.wait_ge(lb_ok, 4)
                dve.wait_ge(set0, 8)

                def blocks(ap, x):
                    return ap.rearrange("q (b x) -> q b x", x=x)

                def prepare(h, p):
                    for d in range(2):
                        dve.wait_ge(evac, NG * h + 4 + 2 * d)
                        dve.tensor_scalar(f1[d][:, :], sg[p][d][:, :], omlb[:, bass.ds(h + NH * d, 1)], TINY,
                                          ALU.mult, ALU.max).then_inc(f_ok, 1)
                    for d in range(2):
                        dve.wait_ge(f_ok, 2 * h + (d + 3))
                        dve.tensor_scalar(kk[d][:, :], f1[d][:, :], -1.0, omlb[:, bass.ds(h + NH * d, 1)],
                                          ALU.mult, ALU.add).then_inc(k_ok, 1)
                    for d in range(2):
                        dve.wait_ge(g_ok, 2 * h + (d + 2))
                        L, C = lat_cols(cum[d]), ctx_cols(cum[d])
                        if d == 1:
                            L, C = cum[d][:, NT - 1:LAT - 1:-1], cum[d][:, TC - 1::-1]
                        dve.tensor_tensor_scan(L, keep[:, :], L, 0.0, ALU.mult, ALU.add)
                        dve.tensor_tensor_scan(C, ones_c[:, :], C, 0.0, ALU.mult, ALU.add).then_inc(cum_ok, 1)
                        dve.wait_ge(cum_ok, 2 * h + (d + 1))
                        L = lat_cols(cum[d])
                        for half, li in LV:
                            v = blocks(L, 2 * half)
                            r = half - 1 if d == 0 else half
                            dve.tensor_tensor(blocks(lev[d][:, li, :], 2 * half), v,
                                              v[:, :, r:r + 1].broadcast_to((P, T // (2 * half), 2 * half)), ALU.subtract)
                        v = blocks(L, 16)
                        dve.tensor_tensor(blocks(dg[d][:, 0, :], 16), v, v[:, :, 8:9].broadcast_to((P, T // 16, 16)), ALU.subtract)
                        for part, x in ((L, HC), (ctx_cols(cum[d]), TC)):
                            v = blocks(part, x)
                            r = x - 1 if d == 0 else 0
                            o = blocks(lat_cols(ks[d]) if x == HC else ctx_cols(ks[d]), x)
                            ins = dve.tensor_tensor(o, v[:, :, r:r + 1].broadcast_to((P, v.shape[1], x)), v, ALU.subtract)
                        ins.then_inc(dif_ok, 1)
                    dve.wait_ge(evac, NG * h + 7)
                    for d in range(2):
                        dve.wait_ge(exp_ok, 2 * h + (d + 1))
                        dve.wait_ge(k_ok, 2 * h + (d + 1))
                        for half, li in LV:
                            v, q, k = (a.rearrange("q (b s t) -> q b s t", s=2, t=half)
                                       for a in (lev[d][:, li, :], qs[p][:, :], lat_cols(kk[d])))
                            for s in range(2):
                                o = v[:, :, s, :]
                                dve.tensor_tensor(o, o, (q if s == 1 - d else k)[:, :, s, :], ALU.mult)
                        dve.tensor_tensor(dg[d][:, 0, :], dg[d][:, 0, :], qs[p][:, :], ALU.mult)
                        dve.tensor_tensor(dg[d][:, 1, :], dg[d][:, 1, :], lat_cols(kk[d]), ALU.mult)
                        dve.tensor_tensor(lat_cols(cum[d]), lat_cols(cum[d]), qs[p][:, :], ALU.mult)
                        dve.tensor_tensor(ks[d][:, :], ks[d][:, :], kk[d][:, :], ALU.mult).then_inc(prod_ok, 1)

                def recur(h, p):
                    for d in range(2):
                        dve.wait_ge(sc_ok, 2 * h + (d + 1))
                        dve.tensor_copy(probe[:, :], SC[:, 0:1])
                        dve.copy_predicated(AT[d][:, :, :], mask[d][:, :].bitcast(U32).unsqueeze(1).broadcast_to((P, NCH, HC)),
                                            SC[:, :].rearrange("q (c t) -> q c t", t=HC)).then_inc(at_ok, 1)
                        dve.wait_ge(kv_ok, 2 * h + (d + 1))
                        c0 = 0 if d == 0 else NCH - 1
                        dve.tensor_copy(S[d][:, c0, :], KV[:, 0:P]).then_inc(s_ok, 1)
                        for n in range(1, NCH):
                            c, last = (n, n - 1) if d == 0 else (NCH - 1 - n, NCH - n)
                            at = last if d == 0 else last - 1
                            dve.wait_ge(s_ok, 8 * h + (4 * d + n))
                            dve.scalar_tensor_tensor(S[d][:, c, :], S[d][:, last, :], dec[d][:, last:last + 1],
                                                     TR[:, at * P:(at + 1) * P], ALU.mult, ALU.add).then_inc(s_ok, 1)
                    dve.wait_ge(rs_ok, h + 1)
                    dve.tensor_tensor(ors[:, :], ors[:, :], OUT[:, :], ALU.mult).then_inc(o1_ok, 1)
                    dve.wait_ge(o1_ok, h + 1)
                    g = K.at["hgrn_g"]
                    dve.scalar_tensor_tensor(hO[:, bass.ds(h, 1), :].rearrange("q a t -> q (a t)"), ors[:, :], K.vec[:, g:g + 1],
                                             gs[p][:, :], ALU.mult, ALU.mult).then_inc(fin_ok, 1)

                with dve.Fori(0, NH // 2) as j:
                    for p in range(2):
                        prepare(2 * j + p, p)
                        recur(2 * j + p, p)


def mat(w, rhs, kt=KD, col=0, step=P, pieces=((0, 0, P),)):
    return w.rearrange("(k p) n -> p k n", p=P), rhs, kt, col, step, pieces


def product_phase(K, tag, mats, iters, on_act, on_dve, freed_by, extra=None):
    G = len(mats)
    n_dma = sum(len(m[5]) for m in mats)
    raws = (4 if mats[0][2] <= KD and iters % 4 == 0 else 2, 2, 1)[G - 1]
    slots = max(raws, 2)
    rights = []
    for m in mats:
        if not any(m[1] is r for r, _ in rights):
            rights.append((m[1], m[2]))
    n_right = sum(kt for _, kt in rights)
    with ExitStack() as st:
        W = [[K.sb(st, f"{tag}_w{s}{g}", [P, mats[g][2], P]) for g in range(G)] for s in range(raws)]
        WH = [[K.sb(st, f"{tag}_wh{s}{g}", [P, mats[g][2], P], F32R) for g in range(G)] for s in range(2)]
        WL = [[K.sb(st, f"{tag}_wl{s}{g}", [P, mats[g][2], P], F32R) for g in range(G)] for s in range(2)]
        RH = [K.sb(st, f"{tag}_rh{r}", [P, kt, T], F32R) for r, (_, kt) in enumerate(rights)]
        RL = [K.sb(st, f"{tag}_rl{r}", [P, kt, T], F32R) for r, (_, kt) in enumerate(rights)]
        of = [next(r for r, (x, _) in enumerate(rights) if x is m[1]) for m in mats]
        ps = K.psum_banks(st, tag)
        sems, old = K.phase()
        w_in, (summed, freed, high, low, r_high, r_low), own = sems[0:raws], sems[4:10], sems[10:]
        groups = iters // slots
        with K.nc.Block() as block:
            @block.sync
            def _(sp):
                clear_old(sp, old)
                with sp.Fori(0, groups) as i:
                    at = {step: sp.snap(i * (slots * step)) for step in {m[4] for m in mats}}
                    for s in range(slots):
                        sp.wait_ge(low, slots * i + (s + 1))
                        for g, (w, _, _, col, step, pieces) in enumerate(mats):
                            for to, off, n in pieces:
                                sp.dma_start(W[s % raws][g][:, :, to:to + n], w[:, :, bass.ds(at[step] + (col + off + s * step), n)])\
                                  .then_inc(w_in[s % raws], 16)

            @block.gpsimd
            def _(pool):
                pool.sem_inc(low, raws)
                with pool.Fori(0, groups) as i:
                    for s in range(slots):
                        pool.wait_ge(high, slots * i + (s + 1))
                        for g in range(G):
                            ins = pool.tensor_tensor(WL[s % 2][g][:, :, :], W[s % raws][g][:, :, :],
                                                     WH[s % 2][g][:, :, :].bitcast(F32), ALU.subtract)
                        ins.then_inc(low, 1)

            @block.tensor
            def _(pe):
                pe.sem_inc(summed, 2)
                pe.wait_ge(r_low, n_right)
                with pe.Fori(0, groups) as i:
                    for s in range(slots):
                        p = s % 2
                        pe.wait_ge(low, slots * i + (s + 1 + raws))
                        pe.wait_ge(freed, slots * i + (s + 1))
                        for g in range(G):
                            kt, rh, rl = mats[g][2], RH[of[g]], RL[of[g]]
                            for k in range(kt):
                                pe.matmul(ps[p * 4 + g][:, :], WH[p][g][:, k, :], rh[:, k, :], start=(k == 0), stop=False)
                                pe.matmul(ps[p * 4 + g][:, :], WH[p][g][:, k, :], rl[:, k, :], start=False, stop=False)
                                ins = pe.matmul(ps[p * 4 + g][:, :], WL[p][g][:, k, :], rh[:, k, :],
                                                start=False, stop=(k == kt - 1))
                        ins.then_inc(summed, 1)

            @block.scalar
            def _(act):
                for r, (x, kt) in enumerate(rights):
                    for k in range(kt):
                        act.activation(RH[r][:, k, :], x[:, k, :], ACT.Copy).then_inc(r_high, 1)

                def weights_high(i, s):
                    act.wait_ge(w_in[s % raws], 16 * n_dma * (slots // raws) * i + 16 * n_dma * (s // raws + 1))
                    act.wait_ge(summed, slots * i + (s + 1))
                    for g in range(G):
                        ins = act.activation(WH[s % 2][g][:, :, :], W[s % raws][g][:, :, :], ACT.Copy)
                    ins.then_inc(high, 1)

                def finish(i, s):
                    if on_act:
                        act.wait_ge(summed, slots * i + (s + 3))
                        on_act(act, slots * i + s, s % 2, ps[s % 2 * 4:s % 2 * 4 + G], freed, own)

                if freed_by == "act":
                    act.sem_inc(freed, 2)
                if extra and "act" in extra:
                    extra["act"](act, own)
                weights_high(0, 0)
                if groups > 1:
                    with act.Fori(0, groups - 1) as i:
                        for s in range(slots):
                            weights_high(i + (s + 1) // slots, (s + 1) % slots)
                            finish(i, s)
                for s in range(slots):
                    if s + 1 < slots:
                        weights_high(groups - 1, s + 1)
                    finish(groups - 1, s)

            @block.vector
            def _(dve):
                n = 0
                for r, (x, kt) in enumerate(rights):
                    for k in range(kt):
                        n += 1
                        dve.wait_ge(r_high, n)
                        dve.tensor_tensor(RL[r][:, k, :], x[:, k, :], RH[r][:, k, :].bitcast(F32), ALU.subtract).then_inc(r_low, 1)
                if freed_by == "dve":
                    dve.sem_inc(freed, 2)
                if extra and "dve" in extra:
                    extra["dve"](dve, own)
                if on_dve:
                    with dve.Fori(0, groups) as i:
                        for s in range(slots):
                            dve.wait_ge(summed, slots * i + (s + 3))
                            on_dve(dve, slots * i + s, s % 2, ps[s % 2 * 4:s % 2 * 4 + G], freed, own)


def tile_at(t, i):
    return t[:, bass.ds(i, 1), :].rearrange("q a t -> q (a t)")


def residual(K, gate, v, bias=None, tmp=None):
    def on_act(act, i, p, banks, freed, own):
        act.activation(tmp[:, p, :], banks[0][:, :], ACT.Identity, bias=K.vec[:, bass.ds(i + bias, 1)]).then_inc(own[0], 1)

    def on_dve(dve, i, p, banks, freed, own):
        if bias is not None:
            dve.wait_ge(own[0], i + 1)
        src = banks[0][:, :] if bias is None else tmp[:, p, :]
        x = tile_at(K.xT, i)
        dve.scalar_tensor_tensor(x, src, K.mod[:, bass.ds(i + gate, 1), v:v + 1].rearrange("q a b -> q (a b)"), x,
                                 ALU.mult, ALU.add).then_inc(freed, 1)
    return (on_act if bias is not None else None), on_dve


CW, CP, GW = 31, 15, 64


def conv_phase(K, u, gate):
    inp = K.inp
    rows = T // GW
    with ExitStack() as st:
        pad = [K.sb(st, f"cv_pad{p}", [P, rows, GW + 2 * CP]) for p in range(2)]
        sig = K.sb(st, "cv_sig", [P, 2, T])
        a_b, dw, dwb = K.at["conv_b_in"], K.at["conv_dw"], K.at["conv_dw_b"]

        def on_act(act, i, p, banks, freed, own):
            act.activation(sig[:, p, :], banks[1][:, :], ACT.Sigmoid, bias=K.vec[:, bass.ds(i + (a_b + 16), 1)]).then_inc(own[0], 1)
            act.activation(tile_at(gate, i), banks[2][:, :], ACT.Silu, bias=K.vec[:, bass.ds(i + (a_b + 32), 1)]).then_inc(own[1], 1)

        def start(dve, own):
            for p in range(2):
                dve.memset(pad[p][:, :, :], 0.0).then_inc(own[2], 1)
            dve.wait_ge(own[2], 2)

        def on_dve(dve, i, p, banks, freed, own):
            dve.wait_ge(own[0], i + 1)
            dve.wait_ge(own[1], i + 1)
            dve.scalar_tensor_tensor(pad[p][:, :, CP:CP + GW], banks[0][:, :].rearrange("q (r t) -> q r t", t=GW),
                                     K.vec[:, bass.ds(i + a_b, 1)], sig[:, p, :].rearrange("q (r t) -> q r t", t=GW),
                                     ALU.add, ALU.mult).then_inc(freed, 1)
            dve.wait_ge(freed, i + 3)
            o = tile_at(u, i).rearrange("q (r t) -> q r t", t=GW)
            dve.tensor_scalar(o, pad[p][:, :, 0:GW], K.vec[:, bass.ds(i + dw, 1)], K.vec[:, bass.ds(i + dwb, 1)],
                              ALU.mult, ALU.add).then_inc(own[3], 1)
            for tap in range(1, CW):
                dve.wait_ge(own[3], CW * i + tap)
                dve.scalar_tensor_tensor(o, pad[p][:, :, tap:tap + GW], K.vec[:, bass.ds(i + (dw + 16 * tap), 1)], o,
                                         ALU.mult, ALU.add).then_inc(own[3], 1)

        w = inp["conv_w_in"][0]
        product_phase(K, "cv", [mat(w, K.hT, col=n * EW) for n in range(3)], EW // P, on_act, on_dve, "dve",
                      extra={"dve": start})


def conv_norm_phase(K, u, gate):
    nc = K.nc
    n = EW // P
    g, b = K.at["conv_ln_g"], K.at["conv_ln_b"]
    with ExitStack() as st:
        mean = K.sb(st, "cn_mean", [P, T])
        rstd = K.sb(st, "cn_rstd", [P, T])
        sq = K.sb(st, "cn_sq", [P, 2, T])
        ps = K.psum_banks(st, "cn")
        sems, old = K.phase()
        sum_ok, mean_ok, cen, squared, var_ok, root, inv, scaled, silu, done = sems[:10]
        with nc.Block() as block:
            @block.sync
            def _(sp):
                clear_old(sp, old)

            @block.tensor
            def _(pe):
                for k in range(n):
                    ins = pe.matmul(ps[0][:, :], K.ones[:, :], u[:, k, :], start=(k == 0), stop=(k == n - 1))
                ins.then_inc(sum_ok, 1)
                for k in range(n):
                    pe.wait_ge(squared, k + 1)
                    pe.matmul(ps[1][:, :], K.ones[:, :], sq[:, k % 2, :], start=(k == 0), stop=(k == n - 1)).then_inc(var_ok, 1)

            @block.vector
            def _(dve):
                dve.wait_ge(sum_ok, 1)
                dve.tensor_scalar(mean[:, :], ps[0][:, :], 1.0 / EW, None, ALU.mult).then_inc(mean_ok, 1)
                dve.wait_ge(mean_ok, 1)
                for k in range(n):
                    dve.tensor_tensor(u[:, k, :], u[:, k, :], mean[:, :], ALU.subtract).then_inc(cen, 1)
                dve.wait_ge(root, 1)
                dve.reciprocal(rstd[:, :], rstd[:, :]).then_inc(inv, 1)
                dve.wait_ge(inv, 1)
                for k in range(n):
                    dve.scalar_tensor_tensor(u[:, k, :], u[:, k, :], K.vec[:, g + k:g + k + 1], rstd[:, :], ALU.mult, ALU.mult).then_inc(scaled, 1)
                for k in range(n):
                    dve.wait_ge(silu, k + 1)
                    dve.tensor_tensor(u[:, k, :], u[:, k, :], gate[:, k, :], ALU.mult).then_inc(done, 1)

            @block.scalar
            def _(act):
                for k in range(n):
                    act.wait_ge(cen, k + 1)
                    if k >= 2:
                        act.wait_ge(var_ok, k - 1)
                    act.activation(sq[:, k % 2, :], u[:, k, :], ACT.Square).then_inc(squared, 1)
                act.wait_ge(var_ok, n)
                act.activation(rstd[:, :], ps[1][:, :], ACT.Sqrt, scale=1.0 / EW, bias=K.epsc[:, 0:1]).then_inc(root, 1)
                for k in range(n):
                    act.wait_ge(scaled, k + 1)
                    act.activation(u[:, k, :], u[:, k, :], ACT.Silu, bias=K.vec[:, b + k:b + k + 1]).then_inc(silu, 1)


def first_block(K):
    inp = K.inp
    norm_phase(K, [(K.xT, K.hT, T, K.at["norm_g"], 0, 8, 0), (K.ctxT, K.ctxT, TC, K.at["norm_g"], 0, 8, 1)])
    with ExitStack() as st:
        hO = K.sb(st, "hgrn_out", [P, NH, T])
        hgrn_phase(K, hO)
        on_act, on_dve = residual(K, 16, 0)
        product_phase(K, "ho", [mat(inp["hgrn_w_out"][0], hO, NH)], KD, on_act, on_dve, "dve")
    K.early.close()
    norm_phase(K, [(K.xT, K.hT, T, K.at["norm_g"] + 8, 24, 32, 0)])
    with ExitStack() as st:
        u = K.sb(st, "conv_u", [P, EW // P, T])
        with ExitStack() as gated:
            gate = K.sb(gated, "conv_gate", [P, EW // P, T])
            conv_phase(K, u, gate)
            conv_norm_phase(K, u, gate)
        tmp = K.sb(st, "co_tmp", [P, 2, T])
        on_act, on_dve = residual(K, 24 + 16, 0, K.at["conv_b_out"], tmp)
        product_phase(K, "co", [mat(inp["conv_w_out"][0], u, EW // P)], KD, on_act, on_dve, "dve")
    norm_phase(K, [(K.xT, K.xT, T, K.at["final_g"], None, None, 0)])


GU, GV, MQ, MV, MO, MI, MF, NQ, NKC, NKS, NVS, NKW, NVW, GA = (0, 512, 1024, 2048, 2560, 3072, 3076, 3080, 3592, 3848,
                                                               3976, 4104, 4232, 4384)
NGATE = 24
NVG = P + NGATE
TT = T // P
MH, DH = 4, 64
NCMP = (T - 32) // 16 + 1
BIG = 1e30
M2 = 48


def token_phase(K, vn, mv, nvs, nvg, gate_rows):
    nc, inp = K.nc, K.inp
    w = inp["w_in_2"][0].rearrange("(k p) n -> p k n", p=P)
    with ExitStack() as st:
        wb = [K.sb(st, f"tk_w{n}", [P, KD, c]) for n, c in enumerate((512, 512, P, NVG, 8))]
        cols = (GV, MV, NVS, NVW, MI)
        lng = K.sb(st, "tk_lng", [P, 512])
        lnb = K.sb(st, "tk_lnb", [P, 512])
        gb = K.sb(st, "tk_gb", [4, 2])
        row = K.sb(st, "tk_sums", [P, 8 * TT])
        sq = K.sb(st, "tk_sq", [P, 512])
        pre = K.sb(st, "tk_pre", [4, 4, T])
        ones_r = K.sb(st, "tk_ones", [4, T])
        BM, NM, IB = gate_rows
        ps = K.psum_banks(st, "tk")
        sems, old = K.phase()
        w_in, (rows_in, mm, ev, a_ok, d_ok, s_ok, gate_ok, gd_ok, t_ok) = sems[:5], sems[5:14]
        with nc.Block() as block:
            @block.sync
            def _(sp):
                clear_old(sp, old)
                for n in range(5):
                    sp.dma_start(wb[n][:, :, :], w[:, :, cols[n]:cols[n] + wb[n].shape[2]]).then_inc(w_in[n], 16)
                sp.dma_start(lng[:, :], inp["gm_ln_g_2"].broadcast_to((P, 512))).then_inc(rows_in, 16)
                sp.dma_start(lnb[:, :], inp["gm_ln_b_2"].broadcast_to((P, 512))).then_inc(rows_in, 16)
                for n in range(2):
                    sp.dma_start(gb[:, n:n + 1], inp["ml_gate_b_2"][0, 4 * n:4 * n + 4].rearrange("(p a) -> p a", a=1)).then_inc(rows_in, 16)

            @block.tensor
            def _(pe):
                n = 0
                for g in range(4):
                    pe.wait_ge(w_in[g], 16)
                    for t in range(TT):
                        if n >= 6:
                            pe.wait_ge(ev, n - 5)
                        c = wb[g].shape[2]
                        for k in range(KD):
                            ins = pe.matmul(ps[n % 6][:, 0:c], K.hT[:, k, t * P:(t + 1) * P], wb[g][:, k, :], start=(k == 0), stop=(k == KD - 1))
                        ins.then_inc(mm, 1)
                        n += 1
                pe.wait_ge(w_in[4], 16)
                for half in range(2):
                    for k in range(KD):
                        ins = pe.matmul(ps[6 + half][0:4, :], wb[4][:, k, 4 * half:4 * half + 4], K.hT[:, k, :], start=(k == 0), stop=(k == KD - 1))
                    ins.then_inc(mm, 1)
                pe.wait_ge(gd_ok, 8)
                pe.wait_ge(ev, 16)
                for t in range(TT):
                    ins = pe.transpose(ps[0][:, 4 * t:4 * t + 4], pre[0:4, 0, t * P:(t + 1) * P], K.ident[0:4, 0:4])
                ins.then_inc(t_ok, 1)

            @block.scalar
            def _(act):
                for t in range(TT):
                    act.wait_ge(mm, t + 1)
                    act.activation(vn[:, t, :], ps[t % 6][:, :], ACT.Gelu_apprx_tanh, accum_out=row[:, t:t + 1]).then_inc(ev, 1)
                for n in range(TT, 4 * TT):
                    act.wait_ge(mm, n + 1)
                    dst = (mv, nvs, nvg)[n // TT - 1]
                    act.activation(dst[:, n % TT, :], ps[n % 6][:, 0:dst.shape[2]], ACT.Copy).then_inc(ev, 1)
                for t in range(TT):
                    act.wait_ge(s_ok, 1)
                    act.activation(sq[:, :], vn[:, t, :], ACT.Square, bias=row[:, 4 + t:5 + t], accum_out=row[:, 8 + t:9 + t]).then_inc(a_ok, 1)
                    act.wait_ge(a_ok, t + 1)
                act.activation(row[:, 12:16], row[:, 8:12], ACT.Sqrt, scale=1.0 / 512, bias=K.epsc[:, 0:1]).then_inc(a_ok, 1)
                act.wait_ge(mm, 4 * TT + 2)
                act.wait_ge(rows_in, 64)
                act.activation(pre[:, 0, :], ps[6][0:4, :], ACT.Identity, bias=gb[:, 0:1]).then_inc(gate_ok, 1)
                act.activation(pre[:, 1, :], ps[7][0:4, :], ACT.Identity, bias=gb[:, 1:2]).then_inc(gate_ok, 1)
                act.wait_ge(gate_ok, 2)
                act.activation(pre[:, 2, :], pre[:, 1, :], ACT.Abs).then_inc(gate_ok, 1)
                act.preload_act_table_set(LOG_EXP_SET)
                act.wait_ge(gate_ok, 3)
                act.activation(pre[:, 2, :], pre[:, 2, :], ACT.Exp, scale=-1.0).then_inc(gate_ok, 1)
                act.wait_ge(gate_ok, 4)
                act.activation(pre[:, 2, :], pre[:, 2, :], ACT.Ln, bias=1.0).then_inc(gate_ok, 1)
                act.wait_ge(ev, 4 * TT)
                act.activation(nvg[:, :, P:NVG], nvg[:, :, P:NVG], ACT.Sigmoid).then_inc(a_ok, 1)

            @block.vector
            def _(dve):
                dve.wait_ge(ev, TT)
                dve.tensor_scalar(row[:, 4:8], row[:, 0:4], -1.0 / 512, None, ALU.mult).then_inc(s_ok, 1)
                dve.memset(ones_r[:, :], 1.0).then_inc(gd_ok, 1)
                dve.wait_ge(rows_in, 64)
                dve.wait_ge(a_ok, 5)
                dve.reciprocal(row[:, 16:20], row[:, 12:16]).then_inc(s_ok, 1)
                dve.wait_ge(s_ok, 2)
                for t in range(TT):
                    v = vn[:, t, :]
                    dve.tensor_scalar(v, v, row[:, 4 + t:5 + t], row[:, 16 + t:17 + t], ALU.add, ALU.mult).then_inc(d_ok, 1)
                    dve.wait_ge(d_ok, 3 * t + 1)
                    dve.tensor_tensor(v, v, lng[:, :], ALU.mult).then_inc(d_ok, 1)
                    dve.wait_ge(d_ok, 3 * t + 2)
                    dve.tensor_tensor(v, v, lnb[:, :], ALU.add).then_inc(d_ok, 1)
                dve.wait_ge(gate_ok, 5)
                dve.scalar_tensor_tensor(pre[:, 3, :], pre[:, 1, :], 0.0, pre[:, 2, :], ALU.min, ALU.subtract).then_inc(gd_ok, 1)
                dve.wait_ge(gd_ok, 2)
                dve.tensor_tensor_scan(pre[:, 1, :], ones_r[:, :], pre[:, 3, :], 0.0, ALU.mult, ALU.add).then_inc(gd_ok, 1)
                dve.tensor_tensor_scan(pre[:, 2, :], pre[:, 3, :], pre[:, 0, :], 0.0, ALU.add, ALU.max).then_inc(gd_ok, 1)
                dve.wait_ge(gd_ok, 4)
                dve.tensor_tensor(BM[:, :], pre[:, 1, :], pre[:, 2, :], ALU.subtract).then_inc(gd_ok, 1)
                dve.tensor_scalar(NM[:, :], pre[:, 2, :], -1.0, None, ALU.mult).then_inc(gd_ok, 1)
                dve.tensor_tensor(ones_r[:, :], pre[:, 0, :], pre[:, 1, :], ALU.subtract).then_inc(gd_ok, 1)
                dve.wait_ge(gd_ok, 7)
                dve.tensor_copy(pre[:, 0, :], ones_r[:, :]).then_inc(gd_ok, 1)
                dve.wait_ge(t_ok, 1)
                dve.tensor_copy(IB[:, :, :], ps[0][:, 0:16].rearrange("q (t h) -> q t h", h=4)).then_inc(d_ok, 1)


def mixer_phase(K, vn, gu):
    nc, inp = K.nc, K.inp
    with ExitStack() as st:
        ws = K.sb(st, "gm_w", [P, 4, P])
        wT = K.sb(st, "gm_wT", [P, 4, P])
        bs = K.sb(st, "gm_bias", [1, 4, P])
        ps = K.psum_banks(st, "gm")
        sems, old = K.phase()
        w_in, tr, wt_ok, mm, done = sems[:5]
        with nc.Block() as block:
            @block.sync
            def _(sp):
                clear_old(sp, old)
                sp.dma_start(ws[:, :, :], inp["gm_ws_2"][0].rearrange("g t s -> t g s")).then_inc(w_in, 16)
                sp.dma_start(bs[:, :, :], inp["gm_bs_2"]).then_inc(w_in, 16)

            @block.tensor
            def _(pe):
                pe.wait_ge(w_in, 32)
                for g in range(4):
                    ins = pe.transpose(ps[0][:, g * P:(g + 1) * P], ws[:, g, :], K.ident[:, :])
                ins.then_inc(tr, 1)
                pe.wait_ge(wt_ok, 1)
                for g in range(4):
                    for c in range(TT):
                        o = ps[1 + g][:, c * P:(c + 1) * P]
                        pe.matmul(o, vn[:, c, g * P:(g + 1) * P], wT[:, g, :], start=True, stop=False)
                        ins = pe.matmul(o, K.ones[0:1, :], bs[:, g, :], start=False, stop=True)
                    ins.then_inc(mm, 1)

            @block.vector
            def _(dve):
                dve.wait_ge(tr, 1)
                dve.tensor_tensor(wT[:, :, :], ps[0][:, :].rearrange("q (g t) -> q g t", t=P),
                                  K.tri[:, :].unsqueeze(1).broadcast_to((P, 4, P)), ALU.mult).then_inc(wt_ok, 1)
                for g in range(4):
                    dve.wait_ge(mm, g + 1)
                    dve.tensor_tensor(gu[:, g, :], gu[:, g, :], ps[1 + g][:, :], ALU.mult).then_inc(done, 1)


def qk_phase(K, qk):
    cw, cb = K.at["ml_w"], K.at["ml_b"]
    with ExitStack() as st:
        pad = K.sb(st, "qk_pad", [P, 2, 3 + T])

        def start(dve, own):
            dve.memset(pad[:, :, 0:3], 0.0).then_inc(own[2], 1)

        def on_act(act, i, p, banks, freed, own):
            act.activation(pad[:, p, 3:3 + T], banks[0][:, :], ACT.Copy).then_inc(freed, 1)
            act.wait_ge(own[0], 4 * i + 4)
            act.activation(tile_at(qk, i), tile_at(qk, i), ACT.Silu).then_inc(own[1], 1)

        def on_dve(dve, i, p, banks, freed, own):
            dve.wait_ge(freed, i + 3)
            o = tile_at(qk, i)
            dve.tensor_scalar(o, pad[:, p, 0:T], K.vec[:, bass.ds(i + cw, 1)], K.vec[:, bass.ds(i + cb, 1)],
                              ALU.mult, ALU.add).then_inc(own[0], 1)
            for tap in range(1, 4):
                dve.wait_ge(own[0], 4 * i + tap)
                dve.scalar_tensor_tensor(o, pad[:, p, tap:tap + T], K.vec[:, bass.ds(i + (cw + 8 * tap), 1)], o,
                                         ALU.mult, ALU.add).then_inc(own[0], 1)

        def start_dve(dve, own):
            start(dve, own)
            dve.wait_ge(own[2], 1)
        product_phase(K, "qk", [mat(K.inp["w_in_2"][0], K.hT, col=MQ)], 8, on_act, on_dve, "act", extra={"dve": start_dve})


def mlstm_phase(K, qk, mv, so, gate_rows):
    nc = K.nc
    BM, NM, IB = gate_rows
    with ExitStack() as st:
        D = K.sb(st, "ml_D", [P, 2, T])
        Pt = K.sb(st, "ml_P", [P, 2, TT, T])
        floor = K.sb(st, "ml_floor", [P, 2, T])
        h = K.sb(st, "ml_h", [P, 2, T])
        sq = K.sb(st, "ml_sq", [P, T])
        rs = K.sb(st, "ml_rs", [P, T])
        ps = K.psum_banks(st, "ml")
        sems, old = K.phase()
        rows, scored, dec, fl, wt, sel, numden, dn, hq, mean, cen, sqd, var, root, inv, fin, expo = sems[:17]
        g = K.at["ml_g"]
        with nc.Block() as block:
            @block.sync
            def _(sp):
                clear_old(sp, old)

            @block.tensor
            def _(pe):
                def weights(a):
                    if a >= 1:
                        pe.wait_ge(dec, 4 * a)
                        pe.wait_ge(fl, a)
                    one = K.ident[0:4, a:a + 1].broadcast_to((4, P))
                    pe.matmul(ps[0][:, :], one, BM[:, :], start=True, stop=True)
                    pe.matmul(ps[1][:, :], one, NM[:, :], start=True, stop=True).then_inc(rows, 1)
                    for j in range(TT):
                        n = TT * a + j
                        if n >= 2:
                            pe.wait_ge(wt, n - 1)
                        pe.matmul(ps[2 + j % 2][:, j * P:T], qk[:, 4 + a, j * P:(j + 1) * P], qk[:, a, j * P:T],
                                  start=True, stop=True).then_inc(scored, 1)

                def values(a):
                    pe.wait_ge(sel, TT * (a + 1))
                    if a >= 1:
                        pe.wait_ge(hq, 4 * a)
                    for o, l in ((ps[4], None), (ps[5], K.ones[:, :])):
                        for j in range(TT):
                            ins = pe.matmul(o[:, j * P:T], mv[:, j, a * P:(a + 1) * P] if l is None else l, Pt[:, a % 2, j, j * P:T],
                                            start=(j == 0), stop=(j == TT - 1))
                    ins.then_inc(numden, 1)

                def norms(a):
                    pe.wait_ge(hq, 4 * a + 4)
                    pe.matmul(ps[6][:, :], K.ones[:, :], h[:, a % 2, :], start=True, stop=True).then_inc(mean, 1)
                    pe.wait_ge(sqd, a + 1)
                    pe.matmul(ps[7][:, :], K.ones[:, :], sq[:, :], start=True, stop=True).then_inc(var, 1)

                for s in range(MH + 2):
                    if s < MH:
                        weights(s)
                    if 1 <= s <= MH:
                        values(s - 1)
                    if s >= 2:
                        norms(s - 2)

            @block.scalar
            def _(act):
                def weights(a):
                    act.wait_ge(rows, a + 1)
                    for j in range(TT):
                        n = TT * a + j
                        act.wait_ge(expo, n + 1)
                        act.activation(D[:, n % 2, j * P:T], D[:, n % 2, j * P:T], ACT.Exp).then_inc(dec, 1)
                    if a >= 2:
                        act.wait_ge(hq, 4 * (a - 1))
                    act.activation(floor[:, a % 2, :], ps[1][:, :], ACT.Exp).then_inc(fl, 1)

                def norms(a):
                    act.wait_ge(cen, a + 1)
                    act.activation(sq[:, :], h[:, a % 2, :], ACT.Square).then_inc(sqd, 1)
                    act.wait_ge(var, a + 1)
                    act.activation(rs[:, :], ps[7][:, :], ACT.Sqrt, scale=1.0 / P, bias=K.epsc[:, 0:1]).then_inc(root, 1)

                for s in range(MH + 2):
                    if s < MH:
                        weights(s)
                    if s >= 2:
                        norms(s - 2)

            @block.gpsimd
            def _(pool):
                for a in range(MH):
                    for j in range(TT):
                        pool.wait_ge(wt, TT * a + j + 1)
                        d = Pt[:, a % 2, j, j * P:(j + 1) * P]
                        pool.affine_select(out=d, in_=d, compare_op=ALU.is_ge, fill=0.0, base=0, pattern=[[1, P]],
                                           channel_multiplier=-1).then_inc(sel, 1)

            @block.vector
            def _(dve):
                def weights(a):
                    if a >= 2:
                        dve.wait_ge(numden, a - 1)
                    for j in range(TT):
                        n = TT * a + j
                        dve.wait_ge(rows, a + 1)
                        dve.tensor_scalar(D[:, n % 2, j * P:T], ps[0][:, j * P:T], IB[:, j, a:a + 1], 0.0, ALU.add, ALU.min).then_inc(expo, 1)
                        dve.wait_ge(scored, n + 1)
                        dve.wait_ge(dec, n + 1)
                        dve.scalar_tensor_tensor(Pt[:, a % 2, j, j * P:T], ps[2 + j % 2][:, j * P:T], float(P) ** -0.5,
                                                 D[:, n % 2, j * P:T], ALU.mult, ALU.mult).then_inc(wt, 1)

                def values(a):
                    dve.wait_ge(numden, a + 1)
                    dve.wait_ge(fl, a + 1)
                    f = floor[:, a % 2, :]
                    dve.tensor_tensor(f, ps[5][:, :], f, ALU.max).then_inc(hq, 1)
                    dve.wait_ge(hq, 4 * a + 1)
                    dve.scalar_tensor_tensor(f, ps[5][:, :], -1.0, f, ALU.mult, ALU.max).then_inc(hq, 1)
                    dve.wait_ge(hq, 4 * a + 2)
                    dve.reciprocal(f, f).then_inc(hq, 1)
                    dve.wait_ge(hq, 4 * a + 3)
                    dve.tensor_tensor(h[:, a % 2, :], ps[4][:, :], f, ALU.mult).then_inc(hq, 1)

                def norms(a):
                    dve.wait_ge(mean, a + 1)
                    x = h[:, a % 2, :]
                    dve.scalar_tensor_tensor(x, ps[6][:, :], -1.0 / P, x, ALU.mult, ALU.add).then_inc(cen, 1)
                    dve.wait_ge(root, a + 1)
                    dve.reciprocal(rs[:, :], rs[:, :]).then_inc(inv, 1)
                    dve.wait_ge(inv, 2 * a + 1)
                    dve.scalar_tensor_tensor(x, x, K.vec[:, g + a:g + a + 1], rs[:, :], ALU.mult, ALU.mult).then_inc(inv, 1)
                    dve.wait_ge(inv, 2 * a + 2)
                    dve.tensor_tensor(so[:, a, :], so[:, a, :], x, ALU.mult).then_inc(fin, 1)

                for s in range(MH + 2):
                    if s < MH:
                        weights(s)
                    if 1 <= s <= MH:
                        values(s - 1)
                    if s >= 2:
                        norms(s - 2)


def compress_phase(K, kvc, kcmp, vcmp):
    nc, inp = K.nc, K.inp
    names = (("nsa_phi_k1_2", "nsa_phi_k2_2", "nsa_pe_k_2"), ("nsa_phi_v1_2", "nsa_phi_v2_2", "nsa_pe_v_2"))
    with ExitStack() as st:
        w1 = [K.sb(st, f"cp_w1{n}", [P, 32, DH]) for n in range(2)]
        w2 = [K.sb(st, f"cp_w2{n}", [P, DH]) for n in range(2)]
        pe_r = K.sb(st, "cp_pe", [32, 2, P])
        peT = K.sb(st, "cp_peT", [P, 2, 32])
        bias = K.sb(st, "cp_bias", [P, 2])
        h1 = K.sb(st, "cp_h1", [P, 2, NCMP])
        ps = K.psum_banks(st, "cp")
        sems, old = K.phase()
        w_in, tr, pt_ok, first, bias_ok, hid, second, done = sems[:8]
        with nc.Block() as block:
            @block.sync
            def _(sp):
                clear_old(sp, old)
                for n, (a, b, c) in enumerate(names):
                    for g in range(2):
                        r = slice(DH * g, DH * g + DH)
                        sp.dma_start(w1[n][r, :, :], inp[a][0].rearrange("(l d) j -> d l j", d=DH)).then_inc(w_in, 16)
                        sp.dma_start(w2[n][r, :], inp[b][0]).then_inc(w_in, 16)
                        sp.dma_start(pe_r[:, n, r], inp[c][0]).then_inc(w_in, 16)

            @block.tensor
            def _(pe):
                pe.wait_ge(w_in, 16 * 12)
                for n in range(2):
                    ins = pe.transpose(ps[4][:, 32 * n:32 * n + 32], pe_r[:, n, :], K.ident[0:32, 0:32])
                ins.then_inc(tr, 1)
                pe.wait_ge(pt_ok, 1)
                for n in range(2):
                    for g in range(2):
                        r = slice(DH * g, DH * g + DH)
                        for bank, of in ((ps[n], lambda l: kvc[r, n, l:l + 16 * (NCMP - 1) + 1:16]), (ps[2 + n], lambda l: peT[r, n, l:l + 1])):
                            c = NCMP if bank is ps[n] else 1
                            for l in range(32):
                                ins = pe.matmul(bank[r, 0:c], w1[n][r, l, :], of(l), start=(l == 0), stop=(l == 31))
                ins.then_inc(first, 1)
                pe.wait_ge(hid, 2)
                for g in range(2):
                    r = slice(DH * g, DH * g + DH)
                    pe.matmul(ps[5][r, 0:NCMP], w2[0][r, :], h1[r, 0, :], start=True, stop=True)
                for g in range(2):
                    r = slice(DH * g, DH * g + DH)
                    ins = pe.matmul(ps[6 + g][0:NCMP, 0:DH], h1[r, 1, :], w2[1][r, :], start=True, stop=True)
                ins.then_inc(second, 1)

            @block.scalar
            def _(act):
                for n in range(2):
                    act.wait_ge(bias_ok, 1)
                    act.activation(h1[:, n, :], ps[n][:, 0:NCMP], ACT.Gelu_apprx_tanh, bias=bias[:, n:n + 1]).then_inc(hid, 1)

            @block.vector
            def _(dve):
                dve.wait_ge(tr, 1)
                dve.tensor_copy(peT[:, :, :], ps[4][:, 0:64].rearrange("q (n l) -> q n l", l=32)).then_inc(pt_ok, 1)
                dve.wait_ge(first, 1)
                dve.tensor_copy(bias[:, 0:1], ps[2][:, 0:1])
                dve.tensor_copy(bias[:, 1:2], ps[3][:, 0:1]).then_inc(bias_ok, 1)
                dve.wait_ge(second, 1)
                dve.tensor_copy(kcmp[:, :], ps[5][:, 0:NCMP]).then_inc(done, 1)
                for g in range(2):
                    dve.tensor_copy(vcmp[0:NCMP, g * DH:(g + 1) * DH], ps[6 + g][0:NCMP, 0:DH]).then_inc(done, 1)


def attention_phase(K, nq, ksw, nvs, nvg, kcmp, vcmp, nO):
    nc = K.nc
    NHD = 8
    SC = DH ** -0.5
    units = [(hd, i) for hd in range(NHD) for i in range(TT)]
    with ExitStack() as st:
        dist = K.sb(st, "at_dist", [P, T])
        distc = K.sb(st, "at_distc", [P, TT, NCMP])
        valid = K.sb(st, "at_valid", [P, TT, NCMP])
        X = K.sb(st, "at_x", [P, 2, 3, T])
        mx = K.sb(st, "at_max", [P, 2, 8])
        PT = K.sb(st, "at_PT", [P, 2, 3, T])
        ps = K.psum_banks(st, "at")
        sems, old = K.phase()
        made, scored, biased, maxed, negd, expd, coef, wtd, turned, copied, summed, out_ok, cmask, mk2 = sems[:14]
        with nc.Block() as block:
            @block.sync
            def _(sp):
                clear_old(sp, old)

            @block.gpsimd
            def _(pool):
                pool.iota(dist[:, :], [[-1, T]], base=T - P, channel_multiplier=1, allow_small_or_imprecise_dtypes=True).then_inc(made, 1)
                pool.iota(distc[:, :, :], [[P, TT], [-16, NCMP]], base=0, channel_multiplier=1, allow_small_or_imprecise_dtypes=True).then_inc(made, 1)
                pool.memset(valid[:, :, :], 1.0).then_inc(made, 1)
                pool.wait_ge(made, 3)
                pool.affine_select(out=dist[:, :], in_=dist[:, :], compare_op=ALU.is_ge, fill=BIG, base=T - P,
                                   pattern=[[-1, T]], channel_multiplier=1).then_inc(made, 1)
                pool.affine_select(out=valid[:, :, :], in_=valid[:, :, :], compare_op=ALU.is_ge, fill=0.0, base=-31,
                                   pattern=[[P, TT], [-16, NCMP]], channel_multiplier=1).then_inc(made, 1)
                pool.tensor_scalar(distc[:, :, :], distc[:, :, :], -15.5, None, ALU.add).then_inc(made, 1)
                pool.wait_ge(made, 6)
                pool.affine_select(out=distc[:, :, :], in_=distc[:, :, :], compare_op=ALU.is_ge, fill=BIG, base=-31,
                                   pattern=[[P, TT], [-16, NCMP]], channel_multiplier=1).then_inc(made, 1)

            @block.tensor
            def _(pe):
                def score(n):
                    hd, i = units[n]
                    g, m = divmod(hd, 4)
                    r = slice(DH * g, DH * g + DH)
                    if n >= 1:
                        pe.wait_ge(biased, 3 * n)
                    q = nq[r, m, i * P:(i + 1) * P]
                    w = (i + 1) * P
                    pe.matmul(ps[0][:, 0:w], q, ksw[r, 1, 0:w], start=True, stop=True)
                    pe.matmul(ps[1][:, 0:w], q, ksw[r, 0, 0:w], start=True, stop=True)
                    pe.matmul(ps[2][:, 0:NCMP], q, kcmp[r, :], start=True, stop=True).then_inc(scored, 1)

                def turn(n):
                    hd, i = units[n]
                    pe.wait_ge(wtd, 3 * n + 3)
                    if n >= 1:
                        pe.wait_ge(copied, 3 * n)
                    for b in range(2):
                        for j in range(i + 1):
                            pe.transpose(ps[3 + b][:, j * P:(j + 1) * P], X[:, n % 2, b, j * P:(j + 1) * P], K.ident[:, :])
                    pe.transpose(ps[5][0:NCMP, 0:P], X[:, n % 2, 2, 0:NCMP], K.ident[:, :]).then_inc(turned, 1)

                def value(n):
                    hd, i = units[n]
                    g = hd // 4
                    pe.wait_ge(copied, 3 * n + 3)
                    if i == 0 and hd >= 2:
                        pe.wait_ge(out_ok, hd - 1)
                    r = slice(DH * (hd % 2), DH * (hd % 2) + DH)
                    o = ps[6 + hd % 2][r, i * P:(i + 1) * P]
                    c = slice(g * DH, (g + 1) * DH)
                    for j in range(i + 1):
                        pe.matmul(o, nvg[:, j, c], PT[:, n % 2, 0, j * P:(j + 1) * P], start=(j == 0), stop=False)
                        pe.matmul(o, nvs[:, j, c], PT[:, n % 2, 1, j * P:(j + 1) * P], start=False, stop=False)
                    pe.matmul(o, vcmp[0:NCMP, c], PT[0:NCMP, n % 2, 2, 0:P], start=False, stop=True).then_inc(summed, 1)

                for s in range(len(units) + 2):
                    if s < len(units):
                        score(s)
                    if 1 <= s <= len(units):
                        turn(s - 1)
                    if s >= 2:
                        value(s - 2)

            @block.vector
            def _(dve):
                def bias(n):
                    hd, i = units[n]
                    slope = -(2.0 ** -(hd + 1)) / SC
                    w = (i + 1) * P
                    dve.wait_ge(scored, n + 1)
                    if n >= 2:
                        dve.wait_ge(turned, n - 1)
                    for b in range(2):
                        dve.scalar_tensor_tensor(X[:, n % 2, b, 0:w], dist[:, T - w:T], slope, ps[b][:, 0:w], ALU.mult, ALU.add).then_inc(biased, 1)
                    dve.scalar_tensor_tensor(X[:, n % 2, 2, 0:NCMP], distc[:, i, :], slope, ps[2][:, 0:NCMP], ALU.mult, ALU.add).then_inc(biased, 1)
                    dve.wait_ge(biased, 3 * n + 3)
                    for b in range(3):
                        ins = dve.tensor_reduce(mx[:, n % 2, b:b + 1], X[:, n % 2, b, 0:w if b < 2 else NCMP], AX.X, ALU.max)
                    ins.then_inc(maxed, 1)
                    dve.wait_ge(maxed, n + 1)
                    dve.tensor_scalar(mx[:, n % 2, 0:3], mx[:, n % 2, 0:3], -SC, None, ALU.mult).then_inc(negd, 1)

                def weigh(n):
                    hd, i = units[n]
                    dve.wait_ge(expd, n + 1)
                    dve.reciprocal(mx[:, n % 2, 3:6], mx[:, n % 2, 3:6]).then_inc(coef, 1)
                    dve.wait_ge(coef, 2 * n + 1)
                    gates = nvg[:, i, P + 3 * hd:P + 3 * hd + 3]
                    dve.tensor_tensor(mx[:, n % 2, 3:6], mx[:, n % 2, 3:6], gates[:, ::-1], ALU.mult).then_inc(coef, 1)
                    dve.wait_ge(coef, 2 * n + 2)
                    w = (i + 1) * P
                    for b in range(2):
                        x = X[:, n % 2, b, 0:w]
                        dve.tensor_scalar(x, x, mx[:, n % 2, 3 + b:4 + b], None, ALU.mult).then_inc(wtd, 1)
                    x = X[:, n % 2, 2, 0:NCMP]
                    dve.scalar_tensor_tensor(x, x, mx[:, n % 2, 5:6], valid[:, i, :], ALU.mult, ALU.mult).then_inc(wtd, 1)

                def out(n):
                    hd, i = units[n]
                    if i == TT - 1:
                        dve.wait_ge(summed, n + 1)
                        r = slice(DH * (hd % 2), DH * (hd % 2) + DH)
                        dve.tensor_copy(nO[r, hd // 2, :], ps[6 + hd % 2][r, :]).then_inc(out_ok, 1)

                dve.wait_ge(made, 7)
                for s in range(len(units) + 2):
                    if s < len(units):
                        bias(s)
                    if 1 <= s <= len(units):
                        weigh(s - 1)
                    if s >= 2:
                        out(s - 2)

            @block.scalar
            def _(act):
                def exps(n):
                    hd, i = units[n]
                    act.wait_ge(negd, n + 1)
                    for b in range(3):
                        x = X[:, n % 2, b, 0:(i + 1) * P if b < 2 else NCMP]
                        ins = act.activation(x, x, ACT.Exp, scale=SC, bias=mx[:, n % 2, b:b + 1], accum_out=mx[:, n % 2, 3 + b:4 + b])
                    ins.then_inc(expd, 1)

                def copies(n):
                    hd, i = units[n]
                    act.wait_ge(turned, n + 1)
                    if n >= 2:
                        act.wait_ge(summed, n - 1)
                    for b in range(2):
                        act.activation(PT[:, n % 2, b, 0:(i + 1) * P], ps[3 + b][:, 0:(i + 1) * P], ACT.Copy).then_inc(copied, 1)
                    act.activation(PT[0:NCMP, n % 2, 2, 0:P], ps[5][0:NCMP, 0:P], ACT.Copy).then_inc(copied, 1)

                for s in range(len(units) + 1):
                    if s < len(units):
                        exps(s)
                    if s >= 1:
                        copies(s - 1)


def act_into(K, dsts, funcs):
    def on_act(act, i, p, banks, freed, own):
        for b, (dst, f) in enumerate(zip(dsts, funcs)):
            ins = act.activation(tile_at(dst, i), banks[b][:, :], f)
        ins.then_inc(freed, 1)
    return on_act


def second_block(K):
    inp = K.inp
    w = inp["w_in_2"][0]
    norm_phase(K, [(K.xT, K.hT, T, K.at["g1_2"], M2, M2 + 8, 2)])
    with ExitStack() as st:
        gu = K.sb(st, "gu", [P, 4, T])
        so = K.sb(st, "ml_o", [P, 4, T])
        nO = K.sb(st, "nsa_o", [P, 4, T])
        product_phase(K, "z1", [mat(w, K.hT, col=GU), mat(w, K.hT, col=MO)], 4,
                      act_into(K, [gu, so], [ACT.Gelu_apprx_tanh, ACT.Sigmoid]), None, "act")
        with ExitStack() as s2:
            mv = K.sb(s2, "ml_v", [P, TT, 512])
            nvs = K.sb(s2, "nsa_vs", [P, TT, P])
            nvg = K.sb(s2, "nsa_vg", [P, TT, NVG])
            rows = (K.sb(s2, "ml_BM", [4, T]), K.sb(s2, "ml_NM", [4, T]), K.sb(s2, "ml_IB", [P, TT, 4]))
            with ExitStack() as s3:
                vn = K.sb(s3, "gm_v", [P, TT, 512])
                token_phase(K, vn, mv, nvs, nvg, rows)
                mixer_phase(K, vn, gu)
            with ExitStack() as s3:
                qk = K.sb(s3, "ml_qk", [P, 8, T])
                qk_phase(K, qk)
                mlstm_phase(K, qk, mv, so, rows)
            with ExitStack() as s3:
                nq = K.sb(s3, "nsa_q", [P, 4, T])
                kvc = K.sb(s3, "nsa_kvc", [P, 2, T])
                ksw = K.sb(s3, "nsa_ksw", [P, 2, T])
                kcmp = K.sb(s3, "nsa_kcmp", [P, NCMP])
                vcmp = K.sb(s3, "nsa_vcmp", [P, P])
                product_phase(K, "nq", [mat(w, K.hT, col=NQ, step=DH, pieces=((0, 0, DH), (DH, 4 * DH, DH)))], 4,
                              act_into(K, [nq], [ACT.Copy]), None, "act")
                product_phase(K, "nk", [mat(w, K.hT, col=NKC), mat(w, K.hT, col=NKS, step=2 * P)], 2,
                              act_into(K, [kvc, ksw], [ACT.Copy, ACT.Copy]), None, "act")
                compress_phase(K, kvc, kcmp, vcmp)
                attention_phase(K, nq, ksw, nvs, nvg, kcmp, vcmp, nO)
        merged = K.hT
        with ExitStack() as s2:
            gates = [K.sb(s2, f"merge_gate{n}", [P, KD, T]) for n in range(3)]
            product_phase(K, "mg", [mat(w, K.hT, col=GA + n * DM) for n in range(3)], KD,
                          act_into(K, gates, [ACT.Sigmoid] * 3), None, "act")
            ups = [mat(inp[f"w_up_{x}_2"][0], y, 4) for x, y in (("a", gu), ("b", so), ("c", nO))]
            product_phase(K, "up", ups, KD, None, merge(gates, merged), "dve")
        on_act, on_dve = residual(K, M2 + 16, 2)
        product_phase(K, "wo2", [mat(inp["w_out_2"][0], merged)], KD, on_act, on_dve, "dve")
    norm_phase(K, [(K.xT, K.hT, T, K.at["g2_2"], M2 + 24, M2 + 32, 2)])
    with ExitStack() as st:
        hid = K.sb(st, "mlp_hid", [P, 32, T])
        rl = K.sb(st, "mlp_relu", [P, 2, T])

        def on_act(act, i, p, banks, freed, own):
            act.wait_ge(own[1], i + 1)
            act.activation(rl[:, p, :], banks[0][:, :], ACT.Relu).then_inc(freed, 1)

        def on_dve(dve, i, p, banks, freed, own):
            dve.wait_ge(freed, i + 3)
            dve.tensor_tensor(tile_at(hid, i), rl[:, p, :], rl[:, p, :], ALU.mult).then_inc(own[1], 1)
        product_phase(K, "m1", [mat(inp["w_mlp1_2"][0], K.hT)], 32, on_act, on_dve, "act",
                      extra={"dve": lambda dve, own: dve.sem_inc(own[1], 2)})
        on_act, on_dve = residual(K, M2 + 40, 2)
        for part in range(4):
            product_phase(K, "m2", [mat(inp["w_mlp2_2"][0][part * DM:(part + 1) * DM], hid[:, part * KD:(part + 1) * KD, :])],
                          KD, on_act, on_dve, "dve")
    norm_phase(K, [(K.xT, K.xT, T, K.at["final_2"], None, None, 2)])


def merge(gates, merged):
    n = len(gates)

    def on_dve(dve, i, p, banks, freed, own):
        m = tile_at(merged, i)
        for b in range(n):
            g = tile_at(gates[b], i)
            dve.tensor_tensor(g, g, banks[b][:, :], ALU.mult).then_inc(own[0], 1)
        dve.wait_ge(own[0], n * i + n)
        dve.tensor_tensor(m, tile_at(gates[0], i), tile_at(gates[1], i), ALU.add).then_inc(own[1] if n == 3 else freed, 1)
        if n == 3:
            dve.wait_ge(own[1], i + 1)
            dve.tensor_tensor(m, m, tile_at(gates[2], i), ALU.add).then_inc(freed, 1)
    return on_dve


M3 = 96
C = 64
NC = T // C
ZC, BC, AC, PB, GTAIL, GLA = 1536, 2048, 2056, 2064, 3856, 3888


def pair_view(t):
    return t.rearrange("q c (h x) -> q c h x", h=2)


def third_constants_phase(K, st):
    nc, inp = K.nc, K.inp
    K.two = K.sb(st, "two_blocks", [P, P])
    K.neg2 = K.sb(st, "neg_blocks", [P, P])
    K.up_s = K.sb(st, "up_strict", [P, P])
    K.up_i = K.sb(st, "up_incl", [P, P])
    K.low_s = K.sb(st, "low_strict", [P, P])
    K.nup_s = K.sb(st, "neg_up_strict", [P, P])
    K.nlow_s = K.sb(st, "neg_low_strict", [P, P])
    K.lvl = K.sb(st, "levels", [P, 6, P])
    K.low0 = K.sb(st, "low_first", [P, P])
    K.stackI = K.sb(st, "stack_ident", [P, C])
    K.keep64 = K.sb(st, "keep64", [P, T])
    K.eps64 = K.sb(st, "eps64", [P, 1])
    sems, old = K.phase()
    made, fixed, last = sems[:3]
    with nc.Block() as block:
        @block.sync
        def _(sp):
            clear_old(sp, old)

        @block.gpsimd
        def _(pool):
            pool.memset(K.two[:, :], 1.0).then_inc(made, 1)
            pool.memset(K.stackI[:, :], 0.0).then_inc(made, 1)
            pool.memset(K.keep64[:, :], 1.0).then_inc(made, 1)
            pool.memset(K.eps64[:, :], 64e-5).then_inc(made, 1)
            pool.memset(K.lvl[:, :, :], 1.0).then_inc(made, 1)
            pool.memset(K.low0[:, :], 1.0).then_inc(made, 1)
            pool.wait_ge(made, 6)
            pool.memset(K.keep64[:, 0:T:C], 0.0).then_inc(fixed, 1)
            n = [1]

            def keep(t, pattern, base, mult, fill=0.0, op=ALU.is_ge):
                pool.wait_ge(fixed, n[0])
                pool.affine_select(out=t, in_=t, compare_op=op, fill=fill, base=base, pattern=pattern,
                                   channel_multiplier=mult).then_inc(fixed, 1)
                n[0] += 1
            two = K.two[:, :].rearrange("q (h x) -> q h x", h=2)
            keep(two, [[-C, 2], [0, C]], 0, 1)
            keep(two, [[C, 2], [0, C]], C - 1, -1)
            keep(K.stackI[:, :], [[-1, C]], 0, 1, 1.0, ALU.not_equal)
            keep(K.stackI[:, :], [[-1, C]], -C, 1, 1.0, ALU.not_equal)
            for l in range(6):
                b = 2 ** l
                v = K.lvl[:, l, :].rearrange("q (g s x) -> q g s x", s=2, x=b)
                keep(v, [[-2 * b, P // (2 * b)], [0, 2], [0, b]], 0, 1)
                keep(v, [[2 * b, P // (2 * b)], [0, 2], [0, b]], b - 1, -1)
                keep(v, [[0, P // (2 * b)], [1, 2], [0, b]], -1, 0)
            v = K.low0[:, :].rearrange("q (g s) -> q g s", s=2)
            keep(v, [[-2, C], [0, 2]], -1, 1)
            keep(v, [[2, C], [0, 2]], 1, -1)
            keep(v, [[0, C], [-1, 2]], 0, 0)
            pool.wait_ge(fixed, n[0])
            pool.tensor_scalar(K.neg2[:, :], K.two[:, :], -1.0, None, ALU.mult).then_inc(last, 1)
            for t in (K.up_s, K.up_i, K.low_s):
                pool.tensor_copy(t[:, :], K.two[:, :]).then_inc(last, 1)
            pool.wait_ge(last, 4)
            keep(K.up_s[:, :], [[1, P]], -1, -1)
            keep(K.up_i[:, :], [[1, P]], 0, -1)
            keep(K.low_s[:, :], [[-1, P]], -1, 1)
            pool.wait_ge(fixed, n[0])
            pool.tensor_scalar(K.nup_s[:, :], K.up_s[:, :], -1.0, None, ALU.mult).then_inc(last, 1)
            pool.tensor_scalar(K.nlow_s[:, :], K.low_s[:, :], -1.0, None, ALU.mult).then_inc(last, 1)


def conv4(K, tag, w, col, iters, dst, cw, stride):
    with ExitStack() as st:
        pad = K.sb(st, tag + "_pad", [P, 2, 3 + T])

        def start(dve, own):
            dve.memset(pad[:, :, 0:3], 0.0).then_inc(own[2], 1)
            dve.wait_ge(own[2], 1)

        def on_act(act, i, p, banks, freed, own):
            act.activation(pad[:, p, 3:3 + T], banks[0][:, :], ACT.Copy).then_inc(freed, 1)
            act.wait_ge(own[0], 4 * i + 4)
            act.activation(tile_at(dst, i), tile_at(dst, i), ACT.Silu).then_inc(own[1], 1)

        def on_dve(dve, i, p, banks, freed, own):
            dve.wait_ge(freed, i + 3)
            o = tile_at(dst, i)
            dve.tensor_scalar(o, pad[:, p, 0:T], K.vec[:, bass.ds(i + cw, 1)], None, ALU.mult).then_inc(own[0], 1)
            for tap in range(1, 4):
                dve.wait_ge(own[0], 4 * i + tap)
                dve.scalar_tensor_tensor(o, pad[:, p, tap:tap + T], K.vec[:, bass.ds(i + (cw + stride * tap), 1)], o,
                                         ALU.mult, ALU.add).then_inc(own[0], 1)
        product_phase(K, tag, [mat(w, K.hT, col=col)], iters, on_act, on_dve, "act", extra={"dve": start})


def shift_phase(K, w, pb):
    mu = K.at["mu"]
    with ExitStack() as st:
        pad = K.sb(st, "sh_pad", [P, 2, 1 + T])
        diff = K.sb(st, "sh_diff", [P, 2, T])

        def start(dve, own):
            dve.memset(pad[:, :, 0:1], 0.0).then_inc(own[2], 1)
            dve.sem_inc(own[1], 2)
            dve.wait_ge(own[2], 1)

        def on_act(act, i, p, banks, freed, own):
            act.wait_ge(own[1], i + 1)
            act.activation(pad[:, p, 1:1 + T], banks[0][:, :], ACT.Copy).then_inc(freed, 1)

        def on_dve(dve, i, p, banks, freed, own):
            dve.wait_ge(freed, i + 3)
            dve.tensor_tensor(diff[:, p, :], pad[:, p, 0:T], pad[:, p, 1:1 + T], ALU.subtract).then_inc(own[0], 1)
            dve.wait_ge(own[0], i + 1)
            dve.scalar_tensor_tensor(tile_at(pb, i), diff[:, p, :], K.vec[:, bass.ds(i + mu, 1)], pad[:, p, 1:1 + T],
                                     ALU.mult, ALU.add).then_inc(own[1], 1)
        product_phase(K, "pb", [mat(w, K.hT, col=PB)], 14, on_act, on_dve, "act", extra={"dve": start})


def gates_phase(K, pb, lw, aa, gg, rows):
    nc, inp = K.nc, K.inp
    w = inp["w_in_3"][0].rearrange("(k p) n -> p k n", p=P)
    with ExitStack() as st:
        wab = K.sb(st, "gt_wab", [P, KD, 16])
        wt = K.sb(st, "gt_wt", [P, KD, 32])
        w2 = K.sb(st, "gt_w2", [C, 512])
        a2 = K.sb(st, "gt_a2", [P, 512])
        g2 = K.sb(st, "gt_g2", [P, 512])
        g2t = K.sb(st, "gt_g2t", [32, 512])
        tail = K.sb(st, "gt_tail", [32, 1 + T])
        tdif = K.sb(st, "gt_tdif", [32, T])
        r = K.sb(st, "gt_rows", [8, 3, T])
        hb = K.sb(st, "gt_hb", [8, 3])
        ps = K.psum_banks(st, "gt")
        sems, old = K.phase()
        w_in, mm, ra, rd, up, upc, z, tdf = sems[:8]
        with nc.Block() as block:
            @block.sync
            def _(sp):
                clear_old(sp, old)
                sp.dma_start(wab[:, :, :], w[:, :, BC:BC + 16]).then_inc(w_in, 16)
                sp.dma_start(wt[:, :, :], w[:, :, GTAIL:GTAIL + 32]).then_inc(w_in, 16)
                sp.dma_start(w2[:, :], inp["w2_3"][0]).then_inc(w_in, 16)
                sp.dma_start(a2[C:P, :], inp["a2_3"][0]).then_inc(w_in, 16)
                sp.dma_start(g2[:, :], inp["g2_3"][0, 0:P, :]).then_inc(w_in, 16)
                sp.dma_start(g2t[:, :], inp["g2_3"][0, P:P + 32, :]).then_inc(w_in, 16)
                sp.dma_start(hb[:, 0:1], inp["a_log_3"].rearrange("a h -> h a")).then_inc(w_in, 16)
                sp.dma_start(hb[:, 1:2], inp["dt_bias_3"].rearrange("a h -> h a")).then_inc(w_in, 16)

            @block.tensor
            def _(pe):
                pe.wait_ge(w_in, 128)
                for n, (o, l) in enumerate(((ps[0][0:8, :], wab[:, :, 0:8]), (ps[1][0:8, :], wab[:, :, 8:16]), (ps[2][0:32, :], wt[:, :, :]))):
                    for k in range(KD):
                        ins = pe.matmul(o, l[:, k, :], K.hT[:, k, :], start=(k == 0), stop=(k == KD - 1))
                    ins.then_inc(mm, 1)
                pe.wait_ge(z, 3)
                for m in range(4):
                    for b in range(3):
                        n = 3 * m + b
                        if n >= 5:
                            pe.wait_ge(upc, n - 4)
                        o, c = ps[3 + n % 5][:, :], slice(m * P, (m + 1) * P)
                        if b == 0:
                            ins = pe.matmul(o, w2[:, c], pb[0:C, 12, :], start=True, stop=True)
                        elif b == 1:
                            ins = pe.matmul(o, a2[C:P, c], pb[C:P, 12, :], start=True, stop=True)
                        else:
                            pe.matmul(o, g2[:, c], pb[:, 13, :], start=True, stop=False)
                            ins = pe.matmul(o, g2t[:, c], tail[:, 1:1 + T], start=False, stop=True)
                        ins.then_inc(up, 1)

            @block.scalar
            def _(act):
                act.wait_ge(mm, 3)
                act.activation(tail[:, 1:1 + T], ps[2][0:32, :], ACT.Copy).then_inc(ra, 1)
                act.activation(pb[0:C, 12, :], pb[0:C, 12, :], ACT.Tanh).then_inc(z, 1)
                act.activation(pb[:, 13, :], pb[:, 13, :], ACT.Sigmoid).then_inc(z, 1)
                act.wait_ge(rd, 2)
                act.activation(tail[:, 1:1 + T], tdif[:, :], ACT.Sigmoid).then_inc(z, 1)
                act.activation(rows[:, 0, :], ps[0][0:8, :], ACT.Sigmoid).then_inc(ra, 1)
                act.activation(r[:, 1, :], ps[1][0:8, :], ACT.Identity, bias=hb[:, 1:2]).then_inc(ra, 1)
                act.wait_ge(ra, 3)
                act.activation(r[:, 2, :], r[:, 1, :], ACT.Abs).then_inc(ra, 1)
                act.preload_act_table_set(LOG_EXP_SET)
                act.wait_ge(ra, 4)
                act.activation(r[:, 2, :], r[:, 2, :], ACT.Exp, scale=-1.0).then_inc(ra, 1)
                act.activation(hb[:, 2:3], hb[:, 0:1], ACT.Exp).then_inc(ra, 1)
                act.wait_ge(ra, 6)
                act.activation(r[:, 2, :], r[:, 2, :], ACT.Ln, bias=1.0).then_inc(ra, 1)
                for m in range(4):
                    w0, a0 = K.at["w0"] + m, K.at["a0"] + m
                    act.wait_ge(up, 3 * m + 3)
                    act.activation(lw[:, m, :], ps[3 + (3 * m) % 5][:, :], ACT.Sigmoid, bias=K.vec[:, w0:w0 + 1]).then_inc(upc, 1)
                    act.activation(aa[:, m, :], ps[3 + (3 * m + 1) % 5][:, :], ACT.Sigmoid, bias=K.vec[:, a0:a0 + 1]).then_inc(upc, 1)
                    act.activation(gg[:, m, :], ps[3 + (3 * m + 2) % 5][:, :], ACT.Copy).then_inc(upc, 1)

            @block.vector
            def _(dve):
                dve.memset(tail[:, 0:1], 0.0)
                dve.memset(hb[:, 2:3], 0.0).then_inc(rd, 1)
                mu = K.at["mu_tail"]
                dve.wait_ge(ra, 1)
                dve.wait_ge(rd, 1)
                dve.tensor_tensor(tdif[:, :], tail[:, 0:T], tail[:, 1:1 + T], ALU.subtract).then_inc(tdf, 1)
                dve.wait_ge(tdf, 1)
                dve.scalar_tensor_tensor(tdif[:, :], tdif[:, :], K.vec[0:32, mu:mu + 1], tail[:, 1:1 + T], ALU.mult, ALU.add).then_inc(rd, 1)
                dve.wait_ge(ra, 7)
                dve.scalar_tensor_tensor(r[:, 1, :], r[:, 1, :], 0.0, r[:, 2, :], ALU.max, ALU.add).then_inc(rd, 1)
                dve.wait_ge(rd, 3)
                dve.tensor_scalar(r[:, 1, :], r[:, 1, :], hb[:, 2:3], -1.0, ALU.mult, ALU.mult).then_inc(rd, 1)
                dve.wait_ge(rd, 4)
                dve.tensor_tensor_scan(rows[:, 1, :], K.keep64[0:8, :], r[:, 1, :], 0.0, ALU.mult, ALU.add).then_inc(rd, 1)


def spread_phase(K, rows, beB, gcB):
    nc = K.nc
    with ExitStack() as st:
        pick = K.sb(st, "sp_pick", [8, 4 * P])
        ps = K.psum_banks(st, "sp")
        sems, old = K.phase()
        made, spread, copied = sems[:3]
        with nc.Block() as block:
            @block.sync
            def _(sp):
                clear_old(sp, old)

            @block.vector
            def _(dve):
                dve.tensor_copy(pick[:, :].rearrange("q (h x) -> q h x", x=C), K.ident[0:8, 0:8].unsqueeze(2).broadcast_to((8, 8, C))).then_inc(made, 1)
                for n in range(8):
                    dve.wait_ge(spread, n + 1)
                    dve.tensor_copy((beB if n % 2 == 0 else gcB)[:, n // 2, :], ps[n][:, :]).then_inc(copied, 1)

            @block.tensor
            def _(pe):
                pe.wait_ge(made, 1)
                for n in range(8):
                    m, row = divmod(n, 2)
                    pe.matmul(ps[n][:, :], pick[:, m * P:(m + 1) * P], rows[:, row, :], start=True, stop=True).then_inc(spread, 1)


def head_norm_phase(K, tag, jobs, eps, mean_of, center=False):
    nc = K.nc
    with ExitStack() as st:
        sq = K.sb(st, tag + "_sq", [P, 2, T])
        rs = K.sb(st, tag + "_rs", [P, 2, T])
        ps = K.psum_banks(st, tag)
        sems, old = K.phase()
        mean, cen, sqd, summed, root, inv, done = sems[:7]
        with nc.Block() as block:
            @block.sync
            def _(sp):
                clear_old(sp, old)

            @block.tensor
            def _(pe):
                if center:
                    for n, (x, _) in enumerate(jobs):
                        if n >= 2:
                            pe.wait_ge(cen, n - 1)
                        pe.matmul(ps[n % 2][:, :], K.two[:, :], x, start=True, stop=True).then_inc(mean, 1)
                for n in range(len(jobs)):
                    pe.wait_ge(sqd, n + 1)
                    if n >= 2:
                        pe.wait_ge(root, n - 1)
                    pe.matmul(ps[2 + n % 2][:, :], K.two[:, :], sq[:, n % 2, :], start=True, stop=True).then_inc(summed, 1)

            @block.scalar
            def _(act):
                def root_of(n):
                    act.wait_ge(summed, n + 1)
                    if n >= 2:
                        act.wait_ge(done, n - 1)
                    act.activation(rs[:, n % 2, :], ps[2 + n % 2][:, :], ACT.Sqrt, scale=1.0 / mean_of, bias=eps[:, 0:1]).then_inc(root, 1)
                for n, (x, _) in enumerate(jobs):
                    if center:
                        act.wait_ge(cen, n + 1)
                    if n >= 2:
                        act.wait_ge(summed, n - 1)
                    act.activation(sq[:, n % 2, :], x, ACT.Square).then_inc(sqd, 1)
                    if n >= 1:
                        root_of(n - 1)
                root_of(len(jobs) - 1)

            @block.vector
            def _(dve):
                if center:
                    for n, (x, _) in enumerate(jobs):
                        dve.wait_ge(mean, n + 1)
                        dve.scalar_tensor_tensor(x, ps[n % 2][:, :], -1.0 / C, x, ALU.mult, ALU.add).then_inc(cen, 1)
                for n, (x, gain) in enumerate(jobs):
                    dve.wait_ge(root, n + 1)
                    dve.reciprocal(rs[:, n % 2, :], rs[:, n % 2, :]).then_inc(inv, 1)
                    dve.wait_ge(inv, n + 1)
                    dve.scalar_tensor_tensor(x, x, gain, rs[:, n % 2, :], ALU.mult, ALU.mult).then_inc(done, 1)


def rwkv_inputs_phase(K, pb, aa, kk, out):
    nc = K.nc
    with ExitStack() as st:
        t = K.sb(st, "ri_t", [P, 4, T])
        ps = K.psum_banks(st, "ri")
        sems, old = K.phase()
        chain, summed, done = sems[:3]
        with nc.Block() as block:
            @block.sync
            def _(sp):
                clear_old(sp, old)

            @block.vector
            def _(dve):
                for m in range(4):
                    r, k = pb[:, m, :], pb[:, 4 + m, :]
                    col = {n: K.vec[:, K.at[n] + m:K.at[n] + m + 1] for n in ("k_k", "k_a", "r_k")}
                    dve.tensor_scalar(kk[:, m, :], k, col["k_k"], None, ALU.mult)
                    dve.tensor_scalar(t[:, m, :], aa[:, m, :], -1.0, col["k_a"], ALU.add, ALU.mult).then_inc(chain, 1)
                    dve.wait_ge(chain, 3 * m + 1)
                    dve.scalar_tensor_tensor(k, t[:, m, :], 1.0, k, ALU.add, ALU.mult).then_inc(chain, 1)
                    dve.wait_ge(chain, 3 * m + 2)
                    dve.scalar_tensor_tensor(t[:, m, :], r, col["r_k"], k, ALU.mult, ALU.mult).then_inc(chain, 1)
                for m in range(4):
                    dve.wait_ge(summed, m + 1)
                    dve.tensor_tensor(out[:, m, :], ps[m][:, :], pb[:, 8 + m, :], ALU.mult).then_inc(done, 1)

            @block.tensor
            def _(pe):
                for m in range(4):
                    pe.wait_ge(chain, 3 * m + 3)
                    pe.matmul(ps[m][:, :], K.two[:, :], t[:, m, :], start=True, stop=True).then_inc(summed, 1)


def delta_phase(K, tag, gdn, src, yT):
    nc = K.nc
    with ExitStack() as st:
        big = lambda n: K.sb(st, f"{tag}_{n}", [P, NC, P])
        stk = lambda n: K.sb(st, f"{tag}_{n}", [P, T])
        Aq, Rq, Bq, Kq = big("Asc"), big("Rsc"), big("Bsc"), None if gdn else big("Ksc")
        As, Rs = (big("Ast"), big("Rst")) if gdn else (Aq, Rq)
        Bh, Kh = big("Bhat"), None if gdn else big("Khat")
        Vb = big("Vb")
        Tm, U, Pm = Bq, (Aq if gdn else Kq), Vb
        AabT, Aab, ArbT = big("AabT"), big("Aab"), big("ArbT")
        AakT, ArkT = (AabT, None) if gdn else (big("AakT"), big("ArkT"))
        M1, M2m, M3m = (big("M1"), big("M2"), big("M3")) if gdn else (None, None, None)
        L, e1, e2, e3, e4, d1, d2 = (stk(n) for n in ("L", "e1", "e2", "e3", "e4", "d1", "d2"))
        gcol = K.sb(st, tag + "_gcol", [P, NC])
        pend = K.sb(st, tag + "_pend", [P, NC])
        V = K.sb(st, tag + "_V", [P, NC, C])
        X = K.sb(st, tag + "_X", [P, C])
        SA = K.sb(st, tag + "_SA", [P, C])
        S = K.sb(st, tag + "_S", [P, C])
        ps = K.psum_banks(st, tag)
        sems, old = K.phase()
        dch, expd, ready, scp, sce, tp, te, vt, vte, xs, xe, ss, se, ys, ye, yc, ns, turn1, turned_c, turn2 = sems[:20]
        st3 = lambda t: t[:, :].rearrange("q (c x) -> q c x", x=C)
        half = lambda t, b: t[:, 4 * b:4 * b + 4, :]
        bank = lambda b: ps[b][:, :].rearrange("q (c x) -> q c x", x=P)
        NSC = 3 if gdn else 5

        def bd(dve, out, x, mask):
            dve.tensor_tensor(pair_view(out[:, :, :]), x.unsqueeze(2).broadcast_to((P, NC, 2, C)),
                              mask.rearrange("q (h x) -> q h x", h=2).unsqueeze(1).broadcast_to((P, NC, 2, C)), ALU.mult)

        with nc.Block() as block:
            @block.sync
            def _(sp):
                clear_old(sp, old)

            @block.vector
            def _(dve):
                with dve.Fori(0, 4) as m:
                    at = lambda t: tile_at(t, m)
                    a3 = lambda t: at(t).rearrange("q (c x) -> q c x", x=C)
                    if gdn:
                        q, k, v, gc, be = src
                        g3 = a3(gc)
                        dve.tensor_tensor(st3(d1), g3, K.stackI[:, :].unsqueeze(1).broadcast_to((P, NC, C)), ALU.mult).then_inc(dch, 1)
                        dve.tensor_tensor(st3(e4), g3[:, :, C - 1:C].broadcast_to((P, NC, C)), g3, ALU.subtract)
                        dve.tensor_copy(L[:, :], at(gc))
                        dve.wait_ge(dch, 6 * m + 1)
                        dve.tensor_reduce(gcol[:, :], st3(d1), AX.X, ALU.add).then_inc(dch, 1)
                        dve.wait_ge(dch, 6 * m + 2)
                        gb = gcol[:, :].unsqueeze(2).broadcast_to((P, NC, C))
                        dve.tensor_tensor(st3(d1), g3, gb, ALU.subtract).then_inc(dch, 1)
                        dve.tensor_tensor(st3(d2), gb, g3, ALU.subtract).then_inc(dch, 1)
                        dve.wait_ge(dch, 6 * m + 4)
                        dve.tensor_scalar(d1[:, :], d1[:, :], 0.0, None, ALU.min).then_inc(dch, 1)
                        dve.tensor_scalar(d2[:, :], d2[:, :], 0.0, None, ALU.min).then_inc(dch, 1)
                        dve.tensor_tensor(e3[:, :], at(k), at(be), ALU.mult).then_inc(ns, 1)
                        bd(dve, Aq, a3(k), K.two[:, :])
                        bd(dve, Rq, a3(q), K.two[:, :])
                        bd(dve, Vb, a3(v), K.two[:, :])
                        dve.wait_ge(expd, m + 1)
                        dve.tensor_tensor(e1[:, :], e2[:, :], at(k), ALU.mult)
                        dve.tensor_tensor(e2[:, :], e2[:, :], at(q), ALU.mult)
                        dve.wait_ge(ns, 2 * m + 1)
                        dve.tensor_tensor(e4[:, :], e4[:, :], e3[:, :], ALU.mult).then_inc(ns, 1)
                        dve.wait_ge(ns, 2 * m + 2)
                        bd(dve, Bq, st3(e3), K.two[:, :])
                        bd(dve, As, st3(e1), K.neg2[:, :])
                        bd(dve, Rs, st3(e2), K.two[:, :])
                        bd(dve, Bh, st3(e4), K.two[:, :])
                        bd(dve, M1, st3(d1), K.nup_s[:, :])
                        bd(dve, M2m, st3(d1), K.up_i[:, :])
                        bd(dve, M3m, st3(d2), K.nlow_s[:, :])
                    else:
                        r, k, v, kk, lw, aa = src
                        dve.tensor_scalar(d1[:, :], at(lw), -float(np.exp(-0.5)), None, ALU.mult).then_inc(dch, 1)
                        dve.wait_ge(dch, 6 * m + 1)
                        dve.tensor_tensor_scan(L[:, :], K.keep64[:, :], d1[:, :], 0.0, ALU.mult, ALU.add).then_inc(dch, 1)
                        dve.wait_ge(dch, 6 * m + 2)
                        dve.tensor_tensor(e1[:, :], L[:, :], d1[:, :], ALU.subtract).then_inc(dch, 1)
                        l3 = st3(L)
                        dve.tensor_tensor(st3(e4), l3[:, :, C - 1:C].broadcast_to((P, NC, C)), l3, ALU.subtract).then_inc(dch, 1)
                        dve.tensor_tensor(d2[:, :], at(kk), at(aa), ALU.mult).then_inc(dch, 2)
                        bd(dve, Vb, a3(v), K.two[:, :])
                        dve.wait_ge(expd, m + 1)
                        dve.wait_ge(dch, 6 * m + 6)
                        dve.tensor_tensor(e1[:, :], e1[:, :], at(kk), ALU.mult)
                        dve.tensor_tensor(e2[:, :], e2[:, :], at(r), ALU.mult)
                        dve.tensor_tensor(d1[:, :], e3[:, :], d2[:, :], ALU.mult)
                        dve.tensor_tensor(e3[:, :], e3[:, :], at(k), ALU.mult)
                        dve.tensor_tensor(d2[:, :], e4[:, :], d2[:, :], ALU.mult)
                        dve.tensor_tensor(e4[:, :], e4[:, :], at(k), ALU.mult).then_inc(ns, 1)
                        dve.wait_ge(ns, m + 1)
                        bd(dve, Aq, st3(e1), K.neg2[:, :])
                        bd(dve, Rq, st3(e2), K.two[:, :])
                        bd(dve, Bq, st3(d1), K.two[:, :])
                        bd(dve, Kq, st3(e3), K.two[:, :])
                        bd(dve, Bh, st3(d2), K.two[:, :])
                        bd(dve, Kh, st3(e4), K.two[:, :])
                    dve.memset(S[:, :], 0.0).then_inc(ready, 1)
                    outs = [(AabT, M1, K.up_s), (Aab, M3m, K.low_s), (ArbT, M2m, K.up_i), (AakT, None, K.up_s), (ArkT, None, K.up_i)][:NSC]
                    for n, (o, mk, const) in enumerate(outs):
                        dve.wait_ge(scp, NSC * m + (n + 1))
                        for b in range(2):
                            mask = half(mk, b) if gdn else const[:, :].unsqueeze(1).broadcast_to((P, 4, P))
                            ins = dve.tensor_tensor(half(o, b), bank(2 * (n % 3) + b), mask, ALU.mult)
                        ins.then_inc(sce, 1)
                    dve.wait_ge(sce, NSC * m + 2)
                    idb = K.ident[:, :].unsqueeze(1).broadcast_to((P, NC, P))
                    dve.tensor_tensor(Tm[:, :, :], Aab[:, :, :], K.low0[:, :].unsqueeze(1).broadcast_to((P, NC, P)), ALU.mult)
                    dve.tensor_tensor(U[:, :, :], AabT[:, :, :], K.lvl[:, 0, :].unsqueeze(1).broadcast_to((P, NC, P)), ALU.mult).then_inc(te, 1)
                    dve.wait_ge(te, 22 * m + 1)
                    dve.tensor_tensor(Tm[:, :, :], Tm[:, :, :], idb, ALU.add)
                    dve.tensor_tensor(U[:, :, :], U[:, :, :], idb, ALU.add).then_inc(te, 1)
                    for l in range(1, 6):
                        for b in range(2):
                            dve.wait_ge(tp, 20 * m + (4 * l - 3 + b))
                            dve.tensor_tensor(half(Pm, b), bank(b), K.lvl[:, l, :].unsqueeze(1).broadcast_to((P, 4, P)),
                                              ALU.mult).then_inc(te, 1)
                        for b in range(2):
                            dve.wait_ge(tp, 20 * m + (4 * l - 1 + b))
                            dve.tensor_tensor(half(U, b), half(U, b), bank(2 + b), ALU.add)
                            dve.tensor_tensor(half(Tm, b), half(Tm, b), bank(4 + b), ALU.add).then_inc(te, 1)
                    for c in range(NC):
                        dve.wait_ge(xs, 2 * NC * m + (2 * c + 1))
                        dve.tensor_copy(X[:, :], ps[0][:, 0:C]).then_inc(xe, 1)
                        dve.wait_ge(xs, 2 * NC * m + (2 * c + 2))
                        if gdn:
                            dve.tensor_tensor(SA[:, :], ps[1][:, 0:C], V[:, c, :], ALU.add).then_inc(xe, 1)
                        else:
                            dve.tensor_copy(SA[:, :], ps[1][:, 0:C]).then_inc(xe, 1)
                        dve.wait_ge(ss, NC * m + (c + 1))
                        dve.scalar_tensor_tensor(S[:, :], S[:, :], pend[:, c:c + 1], ps[3][:, 0:C], ALU.mult, ALU.add).then_inc(se, 1)
                    bdy = pair_view(Vb[:, :, :])
                    dve.tensor_tensor(bdy, ps[2][:, :].rearrange("q (c x) -> q c x", x=C).unsqueeze(2).broadcast_to((P, NC, 2, C)),
                                      K.two[:, :].rearrange("q (h x) -> q h x", h=2).unsqueeze(1).broadcast_to((P, NC, 2, C)),
                                      ALU.mult).then_inc(ye, 1)
                    dve.wait_ge(ys, m + 1)
                    dve.tensor_copy(at(yT), ps[4][:, :]).then_inc(yc, 1)

            @block.scalar
            def _(act):
                with act.Fori(0, 4) as m:
                    act.wait_ge(dch, 6 * m + 6)
                    if gdn:
                        act.activation(e2[:, :], L[:, :], ACT.Exp)
                        act.activation(pend[:, :], L[:, C - 1:T:C], ACT.Exp)
                        act.activation(e4[:, :], e4[:, :], ACT.Exp)
                        act.activation(d1[:, :], d1[:, :], ACT.Exp)
                        act.activation(d2[:, :], d2[:, :], ACT.Exp).then_inc(expd, 1)
                    else:
                        act.activation(e1[:, :], e1[:, :], ACT.Exp)
                        act.activation(e2[:, :], L[:, :], ACT.Exp)
                        act.activation(e3[:, :], L[:, :], ACT.Exp, scale=-1.0)
                        act.activation(pend[:, :], L[:, C - 1:T:C], ACT.Exp)
                        act.activation(e4[:, :], e4[:, :], ACT.Exp).then_inc(expd, 1)
                    act.wait_ge(vt, m + 1)
                    act.activation(V[:, :, :], ps[6][:, :].rearrange("q (c x) -> q c x", x=C), ACT.Copy).then_inc(vte, 1)
                    for n, t in enumerate([Bh] if gdn else [Bh, Kh]):
                        act.wait_ge(turn1, (1 if gdn else 2) * m + (n + 1))
                        act.activation(half(t, 0), bank(7), ACT.Copy).then_inc(turned_c, 1)
                        act.wait_ge(turn2, (1 if gdn else 2) * m + (n + 1))
                        act.activation(half(t, 1), bank(7), ACT.Copy).then_inc(turned_c, 1)

            @block.tensor
            def _(pe):
                hb = 1 if gdn else 2
                with pe.Fori(0, 4) as m:
                    pe.wait_ge(ready, m + 1)
                    prods = [(Bq, Aq), (Aq, Bq), (Bq, Rq), (Kq, Aq), (Kq, Rq)][:NSC]
                    for n, (l, r) in enumerate(prods):
                        if n >= 3:
                            pe.wait_ge(sce, NSC * m + (n - 2))
                        for c in range(NC):
                            ins = pe.matmul(ps[2 * (n % 3) + c // 4][:, (c % 4) * P:(c % 4 + 1) * P], l[:, c, :], r[:, c, :], start=True, stop=True)
                        ins.then_inc(scp, 1)
                    for c in range(NC):
                        ins = pe.matmul(ps[6][:, c * C:(c + 1) * C], Vb[:, c, :], K.stackI[:, :], start=True, stop=True)
                    ins.then_inc(vt, 1)
                    for n, t in enumerate([Bh] if gdn else [Bh, Kh]):
                        for b in range(2):
                            if n > 0 and b == 0:
                                pe.wait_ge(turned_c, 2 * hb * m + 2)
                            if b == 1:
                                pe.wait_ge(turned_c, 2 * hb * m + (2 * n + 1))
                            for c in range(4):
                                ins = pe.transpose(ps[7][:, c * P:(c + 1) * P], t[:, 4 * b + c, :], K.ident[:, :])
                            ins.then_inc(turn1 if b == 0 else turn2, 1)
                    pe.wait_ge(sce, NSC * m + NSC)
                    for l in range(1, 6):
                        for b in range(2):
                            pe.wait_ge(te, 22 * m + (2 if l == 1 else 4 * l - 3 + b))
                            for c in range(4 * b, 4 * b + 4):
                                ins = pe.matmul(ps[b][:, (c % 4) * P:(c % 4 + 1) * P], Aab[:, c, :], U[:, c, :], start=True, stop=True)
                            ins.then_inc(tp, 1)
                        for b in range(2):
                            pe.wait_ge(te, 22 * m + (4 * l - 1 + b))
                            for o, (x, y) in ((2, (Tm, Pm)), (4, (Pm, Tm))):
                                for c in range(4 * b, 4 * b + 4):
                                    ins = pe.matmul(ps[o + b][:, (c % 4) * P:(c % 4 + 1) * P], x[:, c, :], y[:, c, :], start=True, stop=True)
                            ins.then_inc(tp, 1)
                    pe.wait_ge(te, 22 * m + 22)
                    pe.wait_ge(vte, m + 1)
                    pe.wait_ge(turned_c, 2 * hb * m + 2 * hb)
                    for c in range(NC):
                        if c > 0:
                            pe.wait_ge(se, NC * m + c)
                        pe.matmul(ps[0][:, 0:C], As[:, c, :], S[:, :], start=True, stop=False)
                        pe.matmul(ps[0][:, 0:C], AakT[:, c, :], V[:, c, :], start=False, stop=True).then_inc(xs, 1)
                        pe.wait_ge(xe, 2 * NC * m + (2 * c + 1))
                        pe.matmul(ps[1][:, 0:C], U[:, c, :], X[:, :], start=True, stop=True).then_inc(xs, 1)
                        y = ps[2][:, c * C:(c + 1) * C]
                        pe.matmul(y, Rs[:, c, :], S[:, :], start=True, stop=False)
                        if not gdn:
                            pe.matmul(y, ArkT[:, c, :], V[:, c, :], start=False, stop=False)
                            pe.matmul(ps[3][:, 0:C], Kh[:, c, :], V[:, c, :], start=True, stop=False)
                        pe.wait_ge(xe, 2 * NC * m + (2 * c + 2))
                        pe.matmul(y, ArbT[:, c, :], SA[:, :], start=False, stop=True)
                        pe.matmul(ps[3][:, 0:C], Bh[:, c, :], SA[:, :], start=gdn, stop=True).then_inc(ss, 1)
                    pe.wait_ge(ye, m + 1)
                    for c in range(NC):
                        ins = pe.matmul(ps[4][:, c * C:(c + 1) * C], Vb[:, c, :], K.stackI[:, :], start=True, stop=True)
                    ins.then_inc(ys, 1)


def store_phase(K, out):
    nc = K.nc
    with ExitStack() as st:
        o = K.sb(st, "out_tok", [P, TT, DM])
        ps = K.psum_banks(st, "out")
        sems, old = K.phase()
        turned, copied, stored = sems[:3]
        with nc.Block() as block:
            @block.sync
            def _(sp):
                clear_old(sp, old)
                for t in range(TT):
                    sp.wait_ge(copied, 2 * t + 2)
                    sp.dma_start(out[0, t * P:(t + 1) * P, :], o[:, t, :]).then_inc(stored, 16)
                sp.wait_ge(stored, 16 * TT)

            @block.tensor
            def _(pe):
                for n in range(2 * TT):
                    t, h = divmod(n, 2)
                    for k in range(4):
                        ins = pe.transpose(ps[n][:, k * P:(k + 1) * P], K.xT[:, 4 * h + k, t * P:(t + 1) * P], K.ident[:, :])
                    ins.then_inc(turned, 1)

            @block.vector
            def _(dve):
                for n in range(2 * TT):
                    t, h = divmod(n, 2)
                    dve.wait_ge(turned, n + 1)
                    dve.tensor_copy(o[:, t, 512 * h:512 * h + 512], ps[n][:, :]).then_inc(copied, 1)


def ffn_phase(K, hid):
    w = K.inp["w_ffn_in_3"][0]
    cw, n = K.at["ffn_w"], 22
    with ExitStack() as st:
        pad = K.sb(st, "ff_pad", [P, 2, 2 + T])
        conv = K.sb(st, "ff_conv", [P, 2, T])

        def start(dve, own):
            dve.memset(pad[:, :, 0:2], 0.0).then_inc(own[2], 1)
            dve.wait_ge(own[2], 1)

        def on_act(act, i, p, banks, freed, own):
            act.activation(pad[:, p, 2:2 + T], banks[0][:, :], ACT.Copy).then_inc(own[0], 1)
            act.wait_ge(own[1], 3 * i + 3)
            act.activation(conv[:, p, :], conv[:, p, :], ACT.Silu).then_inc(own[3], 1)

        def on_dve(dve, i, p, banks, freed, own):
            dve.wait_ge(own[0], i + 1)
            dve.tensor_scalar(conv[:, p, :], pad[:, p, 0:T], K.vec[:, bass.ds(i + cw, 1)], None, ALU.mult).then_inc(own[1], 1)
            for tap in range(1, 3):
                dve.wait_ge(own[1], 3 * i + tap)
                dve.scalar_tensor_tensor(conv[:, p, :], pad[:, p, tap:tap + T], K.vec[:, bass.ds(i + (cw + n * tap), 1)], conv[:, p, :],
                                         ALU.mult, ALU.add).then_inc(own[1], 1)
            dve.wait_ge(own[3], i + 1)
            dve.tensor_tensor(tile_at(hid, i), conv[:, p, :], banks[1][:, :], ALU.mult).then_inc(freed, 1)
        product_phase(K, "ff", [mat(w, K.hT), mat(w, K.hT, col=n * P)], n, on_act, on_dve, "dve", extra={"dve": start})


def third_block(K):
    inp = K.inp
    w = inp["w_in_3"][0]
    norm_phase(K, [(K.xT, K.hT, T, K.at["g1_3"], M3, M3 + 8, 3)])
    with ExitStack() as st:
        ya = K.sb(st, "gdn_y", [P, 4, T])
        yb = K.sb(st, "rwkv_y", [P, 4, T])
        with ExitStack() as s2:
            third_constants_phase(K, s2)
            lw = K.sb(s2, "rw_lw", [P, 4, T])
            aa = K.sb(s2, "rw_a", [P, 4, T])
            gg = K.sb(s2, "rw_g", [P, 4, T])
            rows = K.sb(s2, "gdn_rows", [8, 2, T])
            with ExitStack() as s3:
                pb = K.sb(s3, "rw_p", [P, 14, T])
                shift_phase(K, w, pb)
                gates_phase(K, pb, lw, aa, gg, rows)
                kk = K.sb(s3, "rw_kk", [P, 4, T])
                bonus = K.sb(s3, "rw_bonus", [P, 4, T])
                rwkv_inputs_phase(K, pb, aa, kk, bonus)
                head_norm_phase(K, "nk3", [(kk[:, m, :], 1.0) for m in range(4)], K.epsc, 1.0)
                r, k, v = pb[:, 0:4, :], pb[:, 4:8, :], pb[:, 8:12, :]
                delta_phase(K, "rw", False, (r, k, v, kk, lw, aa), yb)
                lx = K.at["lnx_w"]
                head_norm_phase(K, "lnx", [(yb[:, m, :], K.vec[:, lx + m:lx + m + 1]) for m in range(4)], K.eps64, float(C), True)
                rwkv_out_phase(K, yb, bonus, gg)
            with ExitStack() as s3:
                gq = K.sb(s3, "gdn_qkv", [P, 12, T])
                gcB = K.sb(s3, "gdn_gc", [P, 4, T])
                beB = K.sb(s3, "gdn_beta", [P, 4, T])
                spread_phase(K, rows, beB, gcB)
                conv4(K, "gq", w, 0, 12, gq, K.at["gdn_w"], 12)
                head_norm_phase(K, "l2", [(gq[:, m, :], C ** -0.5 if m < 4 else 1.0) for m in range(8)], K.epsc, 1.0)
                q, k, v = gq[:, 0:4, :], gq[:, 4:8, :], gq[:, 8:12, :]
                delta_phase(K, "gd", True, (q, k, v, gcB, beB), ya)
            og = K.at["onorm"]
            head_norm_phase(K, "on", [(ya[:, m, :], K.vec[:, og:og + 1]) for m in range(4)], K.epsc, float(C))
            sz = K.sb(s2, "gdn_z", [P, 4, T])
            product_phase(K, "z3", [mat(w, K.hT, col=ZC)], 4, act_into(K, [sz], [ACT.Silu]), None, "act")
            gdn_out_phase(K, ya, sz)
        merged = K.sb(st, "merged3", [P, KD, T])
        with ExitStack() as s2:
            gates = [K.sb(s2, f"merge3_gate{n}", [P, KD, T]) for n in range(2)]
            product_phase(K, "mg3", [mat(w, K.hT, col=GLA + n * DM) for n in range(2)], KD,
                          act_into(K, gates, [ACT.Sigmoid] * 2), None, "act")
            product_phase(K, "up3", [mat(inp["w_branch_gdn_3"][0], ya, 4), mat(inp["w_branch_rwkv_3"][0], yb, 4)], KD,
                          None, merge(gates, merged), "dve")
        on_act, on_dve = residual(K, M3 + 16, 3)
        product_phase(K, "wo3", [mat(inp["w_out_3"][0], merged)], KD, on_act, on_dve, "dve")
    norm_phase(K, [(K.xT, K.hT, T, K.at["g2_3"], M3 + 24, M3 + 32, 3)])
    with ExitStack() as st:
        hid = K.sb(st, "ffn_hid", [P, 22, T])
        ffn_phase(K, hid)
        on_act, on_dve = residual(K, M3 + 40, 3)
        for half in range(2):
            product_phase(K, "fo", [mat(inp["w_ffn_out_3"][0][half * 11 * P:(half + 1) * 11 * P],
                                        hid[:, half * 11:half * 11 + 11, :], 11)], KD, on_act, on_dve, "dve")
    norm_phase(K, [(K.xT, K.xT, T, K.at["final_3"], None, None, 3)])


def rwkv_out_phase(K, yb, bonus, gg):
    nc = K.nc
    sems, old = K.phase()
    chain, done = sems[:2]
    b = K.at["lnx_b"]
    with nc.Block() as block:
        @block.sync
        def _(sp):
            clear_old(sp, old)

        @block.vector
        def _(dve):
            for m in range(4):
                dve.scalar_tensor_tensor(yb[:, m, :], yb[:, m, :], K.vec[:, b + m:b + m + 1], bonus[:, m, :], ALU.add, ALU.add).then_inc(chain, 1)
            dve.wait_ge(chain, 4)
            for m in range(4):
                dve.tensor_tensor(yb[:, m, :], yb[:, m, :], gg[:, m, :], ALU.mult).then_inc(done, 1)


def gdn_out_phase(K, ya, sz):
    nc = K.nc
    sems, old = K.phase()
    with nc.Block() as block:
        @block.sync
        def _(sp):
            clear_old(sp, old)

        @block.vector
        def _(dve):
            for m in range(4):
                dve.tensor_tensor(ya[:, m, :], ya[:, m, :], sz[:, m, :], ALU.mult).then_inc(sems[0], 1)


def program(nc, inp, out):
    with ExitStack() as ctx:
        K = Kit(nc, ctx, inp)
        constants_phase(K)
        modulation_phase(K)
        first_block(K)
        second_block(K)
        third_block(K)
        store_phase(K, out)


_INS = ['x', 'c', 'ctx', 'c_ctx', 'norm_g', 'ada_w', 'ada_b', 'hgrn_w_in', 'hgrn_lb_logits', 'hgrn_norm_g',
        'hgrn_w_out', 'conv_w_in', 'conv_b_in', 'conv_dw', 'conv_dw_b', 'conv_ln_g', 'conv_ln_b',
        'conv_w_out', 'conv_b_out', 'final_norm_g', 'c_2', 'g_norm1_2', 'g_norm2_2', 'w_ada_2', 'b_ada_2',
        'w_in_2', 'gm_ln_g_2', 'gm_ln_b_2', 'gm_ws_2', 'gm_bs_2', 'ml_conv_w_2', 'ml_conv_b_2', 'ml_gate_b_2',
        'ml_norm_g_2', 'nsa_pe_k_2', 'nsa_pe_v_2', 'nsa_phi_k1_2', 'nsa_phi_k2_2', 'nsa_phi_v1_2',
        'nsa_phi_v2_2', 'w_up_a_2', 'w_up_b_2', 'w_up_c_2', 'w_out_2', 'w_mlp1_2', 'w_mlp2_2', 'g_final_2',
        'c_3', 'w_ada_3', 'b_ada_3', 'norm1_w_3', 'w_in_3', 'conv_gdn_3', 'a_log_3', 'dt_bias_3',
        'onorm_gdn_3', 'w_branch_gdn_3', 'mu_rwkv_3', 'w0_3', 'w2_3', 'a0_3', 'a2_3', 'g2_3', 'k_k_3',
        'k_a_3', 'r_k_3', 'lnx_w_3', 'lnx_b_3', 'w_branch_rwkv_3', 'w_out_3', 'norm2_w_3', 'w_ffn_in_3',
        'conv_ffn_3', 'w_ffn_out_3', 'norm_f_w_3']


def kernel(**inputs):
    import concourse.bacc as bacc
    from concourse.bass_utils import run_bass_kernel_spmd

    nc = bacc.Bacc("TRN2", target_bir_lowering=False, num_devices=1)
    arrays, aps = {}, {}
    for name in _INS:
        a = np.ascontiguousarray(inputs[name])
        arrays[f"in_{name}_dram"] = a
        aps[name] = nc.dram_tensor(f"in_{name}_dram", a.shape, mybir.dt.from_np(a.dtype), kind="ExternalInput").ap()
    out = nc.dram_tensor("out_dram", (1, T, DM), F32, kind="ExternalOutput").ap()
    program(nc, aps, out)
    return run_bass_kernel_spmd(nc, [arrays], core_ids=[0]).results[0]["out_dram"]
```
